# Optimizing a Trainium2 kernel written in Bass

```python
import jax, jax.numpy as jnp
from jax import lax
import numpy as np

D_MODEL = 1024
BATCH = 1
SEQ = 256
DEPTH = 2
DEC_BATCH = 8
DEC_SEQ = 4
PAST_LEN = 2048
PAGE_SIZE = 128

N_MIXERS = 2
N_CONV_LAYERS = (DEPTH + N_MIXERS - 1) // N_MIXERS
N_RET_LAYERS = DEPTH // N_MIXERS
CONV_DIM = D_MODEL
CONV_WIDTH = 3
RET_HEADS = 4
RET_DK = D_MODEL // RET_HEADS
RET_DV = 2 * RET_DK
RET_CHUNK = 128
ROPE_BASE = 10000.0
N_MEM = 256
XA_HEADS = 4
XA_DIM = D_MODEL // XA_HEADS
XA_WIDTH = XA_HEADS * XA_DIM
N_GROUPS = 4
EXPERTS_PER_GROUP = 8
N_EXPERTS = N_GROUPS * EXPERTS_PER_GROUP
TOP_K_IN_GROUP = 2
EXPERT_FF = 256
EPS = 1e-6

CONV_MIX_W = 3 * CONV_DIM
CONV_IN = CONV_MIX_W + XA_WIDTH
CONV_OUT_IN = CONV_DIM + XA_WIDTH
RET_MIX_W = 2 * RET_HEADS * RET_DK + 2 * RET_HEADS * RET_DV
RET_IN = RET_MIX_W + XA_WIDTH
RET_OUT_IN = RET_HEADS * RET_DV + XA_WIDTH

kernel_name = 'hybrid_conv_retention_hmoe_step'

def rmsnorm(x, g):
    xf = x.astype(jnp.float32)
    y = xf * lax.rsqrt(jnp.mean(xf * xf, axis=-1, keepdims=True) + EPS) * g.astype(jnp.float32)
    return y.astype(x.dtype)

def rotary(x, pos):
    half = x.shape[-1] // 2
    inv = ROPE_BASE ** (-jnp.arange(half, dtype=jnp.float32) / half)
    ang = pos.astype(jnp.float32)[:, None] * inv[None, :]
    cos = jnp.cos(ang)[None, :, None, :]
    sin = jnp.sin(ang)[None, :, None, :]
    x1, x2 = x[..., :half], x[..., half:]
    return jnp.concatenate([x1 * cos - x2 * sin, x1 * sin + x2 * cos], axis=-1)

def causal_conv(u, state, w):
    T = u.shape[1]
    full = jnp.concatenate([state.astype(u.dtype), u], axis=1)
    y = sum(w[k].astype(u.dtype) * full[:, k:k + T] for k in range(CONV_WIDTH))
    return y, full[:, T:]

def conv_mixer(z, state, w):
    b_gate = z[..., :CONV_DIM]
    c_gate = z[..., CONV_DIM:2 * CONV_DIM]
    v = z[..., 2 * CONV_DIM:3 * CONV_DIM]
    y, new_state = causal_conv(c_gate * v, state, w)
    return b_gate * y, new_state

def retention_scan(q, k, v, s0, log_g):
    B, T = q.shape[0], q.shape[1]
    L = RET_CHUNK if T % RET_CHUNK == 0 else T
    n = T // L
    idx = jnp.arange(L)
    diff = idx[:, None] - idx[None, :]
    decay = jnp.where(diff[None] >= 0,
                      jnp.exp(jnp.maximum(diff, 0)[None].astype(jnp.float32) * log_g[:, None, None]),
                      0.0)
    inner = jnp.exp((idx + 1).astype(jnp.float32)[:, None] * log_g[None, :])
    tail = jnp.exp((L - 1 - idx).astype(jnp.float32)[:, None] * log_g[None, :])
    full = jnp.exp(L * log_g)

    def to_chunks(a):
        return jnp.moveaxis(a.reshape((B, n, L) + a.shape[2:]), 1, 0)

    def step(s, qkv):
        qc, kc, vc = qkv
        scores = jnp.einsum('blhd,bmhd->bhlm', qc, kc) * decay[None]
        o_intra = jnp.einsum('bhlm,bmhe->blhe', scores, vc)
        o_cross = jnp.einsum('blhd,bhde->blhe', qc, s) * inner[None, :, :, None]
        s_new = full[None, :, None, None] * s + jnp.einsum(
            'blhd,blhe->bhde', kc * tail[None, :, :, None], vc)
        return s_new, o_intra + o_cross

    s_fin, o = lax.scan(step, s0, (to_chunks(q), to_chunks(k), to_chunks(v)))
    o = jnp.moveaxis(o, 0, 1).reshape(B, T, RET_HEADS, RET_DV)
    return o, s_fin

def retention_mixer(z, state, pos, gn_g):
    B, T = z.shape[0], z.shape[1]
    qd = RET_HEADS * RET_DK
    vd = RET_HEADS * RET_DV
    q = z[..., :qd].reshape(B, T, RET_HEADS, RET_DK).astype(jnp.float32)
    k = z[..., qd:2 * qd].reshape(B, T, RET_HEADS, RET_DK).astype(jnp.float32)
    v = z[..., 2 * qd:2 * qd + vd].reshape(B, T, RET_HEADS, RET_DV).astype(jnp.float32)
    g = z[..., 2 * qd + vd:2 * qd + 2 * vd].astype(jnp.float32)
    q = rotary(q, pos)
    k = rotary(k, pos) * (RET_DK ** -0.5)
    log_g = jnp.log1p(-jnp.exp2(-5.0 - jnp.arange(RET_HEADS, dtype=jnp.float32)))
    o, s_new = retention_scan(q, k, v, state.astype(jnp.float32), log_g)
    mu = jnp.mean(o, axis=-1, keepdims=True)
    var = jnp.mean(jnp.square(o - mu), axis=-1, keepdims=True)
    o = ((o - mu) * lax.rsqrt(var + EPS)).reshape(B, T, vd) * gn_g.astype(jnp.float32)
    return (jax.nn.silu(g) * o).astype(z.dtype), s_new

def cross_attn(q, mem_k, mem_v):
    B, T = q.shape[0], q.shape[1]
    s = jnp.einsum('bthd,bmhd->bhtm', q.astype(jnp.float32), mem_k.astype(jnp.float32)) * (XA_DIM ** -0.5)
    p = jax.nn.softmax(s, axis=-1)
    o = jnp.einsum('bhtm,bmhd->bthd', p, mem_v.astype(jnp.float32))
    return o.reshape(B, T, XA_WIDTH).astype(q.dtype)

def hier_moe(h, w_group, w_router, w_gate_up, w_down):
    def one_seq(hs):
        hf = hs.astype(jnp.float32)
        lg = hf @ w_group.astype(jnp.float32)
        pg = jax.nn.softmax(lg, axis=-1)
        g = jnp.argmax(lg, axis=-1)
        pg_sel = jnp.take_along_axis(pg, g[:, None], axis=1)[:, 0]
        le = (hf @ w_router.astype(jnp.float32)).reshape(-1, N_GROUPS, EXPERTS_PER_GROUP)
        sel = jnp.take_along_axis(le, g[:, None, None], axis=1)[:, 0]
        pe = jax.nn.softmax(sel, axis=-1)
        topv, topi = lax.top_k(pe, TOP_K_IN_GROUP)
        wts = topv / jnp.sum(topv, axis=-1, keepdims=True) * pg_sel[:, None]
        eidx = g[:, None] * EXPERTS_PER_GROUP + topi
        gate = jnp.sum(jax.nn.one_hot(eidx, N_EXPERTS, dtype=jnp.float32) * wts[..., None], axis=1)
        gu = jnp.einsum('td,edf->tef', hs, w_gate_up)
        act = jax.nn.silu(gu[..., :EXPERT_FF]) * gu[..., EXPERT_FF:] * gate[..., None].astype(hs.dtype)
        return jnp.einsum('tef,efd->td', act, w_down)
    return lax.map(one_seq, h)

def trunk(x, pos, conv_states, ret_states, mem_ks, mem_vs, norm_mix, norm_ffn, conv_w_in, conv_w,
          conv_w_out, ret_w_in, ret_gn, ret_w_out, moe_w_group, moe_w_router, moe_w_gate_up,
          moe_w_down, final_norm):
    B, T = x.shape[0], x.shape[1]
    new_conv, new_ret = [], []
    for i in range(DEPTH):
        h = rmsnorm(x, norm_mix[i])
        j = i // N_MIXERS
        if i % N_MIXERS == 0:
            z = h @ conv_w_in[j]
            mix, ns = conv_mixer(z[..., :CONV_MIX_W], conv_states[j], conv_w[j])
            new_conv.append(ns)
            q_x = z[..., CONV_MIX_W:]
            w_out = conv_w_out[j]
        else:
            z = h @ ret_w_in[j]
            mix, ns = retention_mixer(z[..., :RET_MIX_W], ret_states[j], pos, ret_gn[j])
            new_ret.append(ns)
            q_x = z[..., RET_MIX_W:]
            w_out = ret_w_out[j]
        xa = cross_attn(q_x.reshape(B, T, XA_HEADS, XA_DIM), mem_ks[i], mem_vs[i])
        x = x + jnp.concatenate([mix, xa], axis=-1) @ w_out
        x = x + hier_moe(rmsnorm(x, norm_ffn[i]), moe_w_group[i], moe_w_router[i],
                         moe_w_gate_up[i], moe_w_down[i])
    return rmsnorm(x, final_norm), jnp.stack(new_conv), jnp.stack(new_ret)

def setup_inputs(seed: int = 0) -> dict:
    key = jax.random.key(seed)
    ks = jax.random.split(key, 24)
    f32 = jnp.float32

    def nrm(k, shape, scale):
        return jax.random.normal(k, shape, f32) * scale

    return {
        'x_prompt': nrm(ks[0], (BATCH, SEQ, D_MODEL), 1.0),
        'x_sample': nrm(ks[1], (DEC_BATCH, DEC_SEQ, D_MODEL), 1.0),
        'state_conv': nrm(ks[2], (N_CONV_LAYERS, DEC_BATCH, CONV_WIDTH - 1, CONV_DIM), 1.0),
        'state_ret': nrm(ks[3], (N_RET_LAYERS, DEC_BATCH, RET_HEADS, RET_DK, RET_DV), 0.25),
        'cache_mem_k': nrm(ks[4], (DEPTH, DEC_BATCH, N_MEM, XA_HEADS, XA_DIM), 1.0),
        'cache_mem_v': nrm(ks[5], (DEPTH, DEC_BATCH, N_MEM, XA_HEADS, XA_DIM), 1.0),
        'mem_prompt': nrm(ks[6], (BATCH, N_MEM, D_MODEL), 1.0),
        'norm_mix': 1.0 + nrm(ks[7], (DEPTH, D_MODEL), 0.02),
        'norm_ffn': 1.0 + nrm(ks[8], (DEPTH, D_MODEL), 0.02),
        'mem_norm': 1.0 + nrm(ks[9], (DEPTH, D_MODEL), 0.02),
        'w_mem_kv': nrm(ks[10], (DEPTH, D_MODEL, 2 * XA_WIDTH), D_MODEL ** -0.5),
        'conv_w_in': nrm(ks[11], (N_CONV_LAYERS, D_MODEL, CONV_IN), D_MODEL ** -0.5),
        'conv_w': nrm(ks[12], (N_CONV_LAYERS, CONV_WIDTH, CONV_DIM), CONV_WIDTH ** -0.5),
        'conv_w_out': nrm(ks[13], (N_CONV_LAYERS, CONV_OUT_IN, D_MODEL), CONV_OUT_IN ** -0.5),
        'ret_w_in': nrm(ks[14], (N_RET_LAYERS, D_MODEL, RET_IN), D_MODEL ** -0.5),
        'ret_gn': 1.0 + nrm(ks[15], (N_RET_LAYERS, RET_HEADS * RET_DV), 0.02),
        'ret_w_out': nrm(ks[16], (N_RET_LAYERS, RET_OUT_IN, D_MODEL), RET_OUT_IN ** -0.5),
        'moe_w_group': nrm(ks[17], (DEPTH, D_MODEL, N_GROUPS), D_MODEL ** -0.5),
        'moe_w_router': nrm(ks[18], (DEPTH, D_MODEL, N_EXPERTS), D_MODEL ** -0.5),
        'moe_w_gate_up': nrm(ks[19], (DEPTH, N_EXPERTS, D_MODEL, 2 * EXPERT_FF), D_MODEL ** -0.5),
        'moe_w_down': nrm(ks[20], (DEPTH, N_EXPERTS, EXPERT_FF, D_MODEL), EXPERT_FF ** -0.5),
        'final_norm': 1.0 + nrm(ks[21], (D_MODEL,), 0.02),
    }

def reference(x_prompt, x_sample, state_conv, state_ret, cache_mem_k, cache_mem_v, mem_prompt,
              norm_mix, norm_ffn, mem_norm, w_mem_kv, conv_w_in, conv_w, conv_w_out, ret_w_in,
              ret_gn, ret_w_out, moe_w_group, moe_w_router, moe_w_gate_up, moe_w_down, final_norm):
    B = x_prompt.shape[0]
    mk, mv = [], []
    for i in range(DEPTH):
        kv = rmsnorm(mem_prompt, mem_norm[i]) @ w_mem_kv[i]
        mk.append(kv[..., :XA_WIDTH].reshape(B, N_MEM, XA_HEADS, XA_DIM))
        mv.append(kv[..., XA_WIDTH:].reshape(B, N_MEM, XA_HEADS, XA_DIM))
    mem_k_prompt = jnp.stack(mk)
    mem_v_prompt = jnp.stack(mv)

    pos_prompt = jnp.arange(SEQ, dtype=jnp.int32)
    pos_sample = PAST_LEN + jnp.arange(DEC_SEQ, dtype=jnp.int32)
    conv0 = [jnp.zeros((B, CONV_WIDTH - 1, CONV_DIM), x_prompt.dtype) for _ in range(N_CONV_LAYERS)]
    ret0 = [jnp.zeros((B, RET_HEADS, RET_DK, RET_DV), jnp.float32) for _ in range(N_RET_LAYERS)]

    y_prompt, conv_prompt, ret_prompt = trunk(
        x_prompt, pos_prompt, conv0, ret0,
        [mem_k_prompt[i] for i in range(DEPTH)], [mem_v_prompt[i] for i in range(DEPTH)],
        norm_mix, norm_ffn, conv_w_in, conv_w, conv_w_out, ret_w_in, ret_gn, ret_w_out,
        moe_w_group, moe_w_router, moe_w_gate_up, moe_w_down, final_norm)
    y_sample, conv_sample, ret_sample = trunk(
        x_sample, pos_sample,
        [state_conv[j] for j in range(N_CONV_LAYERS)], [state_ret[j] for j in range(N_RET_LAYERS)],
        [cache_mem_k[i] for i in range(DEPTH)], [cache_mem_v[i] for i in range(DEPTH)],
        norm_mix, norm_ffn, conv_w_in, conv_w, conv_w_out, ret_w_in, ret_gn, ret_w_out,
        moe_w_group, moe_w_router, moe_w_gate_up, moe_w_down, final_norm)
    return (y_prompt, y_sample, conv_prompt, conv_sample, ret_prompt, ret_sample, mem_k_prompt, mem_v_prompt)


_drawn_inputs = setup_inputs


def setup_inputs(seed=0):
    import zlib

    import numpy as np

    out = dict(_drawn_inputs(seed))
    spreads = {}
    factors = {'mem_norm': 2.768, 'ret_gn': 3.099, 'final_norm': 2.752}
    for name, (base, spread) in spreads.items():
        noise = np.random.default_rng([zlib.crc32(name.encode()), seed]).standard_normal(out[name].shape)
        drawn = base * np.exp(spread * noise) if base else spread * noise
        out[name] = __import__('jax').numpy.asarray(drawn.astype(out[name].dtype))
    for name, factor in factors.items():
        out[name] = (out[name] * factor).astype(out[name].dtype)
    return out
```

```python
from contextlib import ExitStack

import numpy as np

import concourse.bass as bass
from concourse import mybir

F32 = mybir.dt.float32
I32 = mybir.dt.int32
U32 = mybir.dt.uint32
ALU = mybir.AluOpType
ACT = mybir.ActivationFunctionType
AX = mybir.AxisListType

P = 128
D = 1024
KD = D // P
TP, NB, NS = 256, 8, 4
TD = NB * NS
T = TP + TD
PAST = 2048
NM = 256
H = 4
DV = 512
FF = 256
NE, NG = 32, 4
EPG = NE // NG
EPS = 1e-6
SLOT = 4096
R = 6
CAP = 64
PASSES = -(-T // CAP)
PAIRS = NE // 2
LROW = PASSES * CAP * PAIRS
FAR = 1 << 20
BIG = 3.0e38
BLK = [(0, 128), (128, 128), (256, 32)]
LOGG = [float(np.log1p(-np.exp2(-5.0 - h))) for h in range(H)]

SEQ_A = ([("kv0", c) for c in range(4)] + [("cin", c) for c in range(8)] + [("kc0", c) for c in range(4)]
         + [("vc0", c) for c in range(4)] + [("cout", c) for c in range(4)] + [("kv1", c) for c in range(4)])
SEQ_B = ([("rin", c) for c in range(14)] + [("st", c) for c in range(8)]
         + [("kc1", c) for c in range(4)] + [("vc1", c) for c in range(4)] + [("rout", c) for c in range(8)])
OFF_A = 0
OFF_M0 = len(SEQ_A) % R
OFF_B = OFF_M0
OFF_M1 = (OFF_B + len(SEQ_B)) % R


def constant_columns():
    cols = [("ident", P), ("ones", P), ("tri", P), ("iota", NE), ("cexp", NE), ("cos", T), ("sin", T),
            ("decay", H * P), ("dmask", TD), ("inner", H * P), ("tail", H), ("tdec", 1), ("kvmask", NB * H),
            ("neghalf", 1), ("eps", 1), ("valid", 3), ("far", 3), ("thr", 4), ("tok", 6), ("pair", 6)]
    at, out = 0, {}
    for n, w in cols:
        out[n] = (at, w)
        at += w
    return out, at


def parameter_columns():
    cols = [("mix0", 8), ("mix1", 8), ("ffn0", 8), ("ffn1", 8), ("mem0", 8), ("mem1", 8), ("final", 8),
            ("gn", 16), ("cw", 24)]
    at, out = 0, {}
    for n, w in cols:
        out[n] = (at, w)
        at += w
    return out, at


CC, NCC = constant_columns()
PC, NPC = parameter_columns()


def build(nc, a):
    dram_h = [nc.dram_tensor(f"normed_tokens{i}", (T, D), F32).ap() for i in range(2)]
    dram_y = [nc.dram_tensor(f"expert_rows{i}", (2 * T, D), F32).ap() for i in range(2)]
    dram_l = [nc.dram_tensor(f"expert_lists{i}", (2 * LROW, 3), I32).ap() for i in range(2)]

    with ExitStack() as ctx:
        def sb(name, words, dt=F32):
            return ctx.enter_context(nc.sbuf_tensor(name, [P, words], dt))

        sems = {}

        def S(name):
            if name not in sems:
                sems[name] = ctx.enter_context(nc.semaphore(name))
            return sems[name]

        ring = sb("ring", R * SLOT)
        cst = sb("cst", NCC)
        par = sb("par", NPC)
        xT_ = sb("xT", KD * T)
        hT_ = sb("hT", KD * T)
        small = sb("small", 96)
        arena = sb("arena", 21568)
        bank = [ctx.enter_context(nc.psum_tensor(f"bank{i}", [P, 512], F32)) for i in range(8)]

        def C(name, rows=P):
            o, w = CC[name]
            return cst[0:rows, o:o + w]

        def G(name):
            o, w = PC[name]
            return par[:, o:o + w]

        def ar(off, n):
            return arena[:, off:off + n]

        def v3(ap, k):
            return ap.rearrange("p (k t) -> p k t", k=k)

        HM1, KTO, VO, SQO, CATO, PHO, QMO, MSO = 0, 2048, 4096, 6144, 8448, 15360, 18688, 20992
        xT, hT = v3(xT_[:, :], KD), v3(hT_[:, :], KD)
        hm1 = v3(ar(HM1, KD * NM), KD)
        KT = v3(ar(KTO, 2048), 8)
        V = v3(ar(VO, 2048), 2)
        sq = v3(ar(SQO, KD * T), KD)
        cat = v3(ar(CATO, 24 * T), 24)
        memT = v3(ar(CATO, KD * NM), KD)
        hm0 = v3(ar(CATO + 2048, KD * NM), KD)
        Ktok = v3(ar(PHO, 2048), 2)
        keys1, values1 = v3(hT_[:, 0:2048], 2), v3(ar(SQO, 2048), 2)
        qx = v3(ar(PHO, 8 * T), 8)
        qm_ = ar(QMO, 8 * T)
        qm = v3(qm_, 8)
        qm_diag = qm.rearrange("p h (b x) -> p h b x", x=TD + NS)[:, :, :, 0:NS]
        c_sb = [ar(SQO + 288 * i, T) for i in range(2)]
        full = [ar(SQO + 576 + 306 * i, 306) for i in range(2)]
        yc = [ar(SQO + 1188 + 288 * i, T) for i in range(2)]
        stc = v3(ar(PHO + 2304, 128), 8)
        cvp = v3(ar(PHO + 2432, 16), 8)
        cvs = v3(ar(PHO + 2448, 128), 8)
        Pm = [hT_[:, 256 * i:256 * i + 256] for i in range(2)]
        PT = [v3(hT_[:, 512 + 512 * i:1024 + 512 * i], 2) for i in range(2)]
        od = hT_[:, 1536:1792]
        mx, nb_, rs, rr = (small[:, 9 * i:9 * i + 9] for i in range(4))
        qTh, kTh = v3(ar(PHO, 576), 2), v3(ar(PHO + 576, 576), 2)
        vTh = v3(ar(PHO + 1152, 1152), 4)
        vtok = v3(ar(PHO + 2304, 1024), 2)
        kvar = [ar(PHO + 2304 + 256 * i, 256) for i in range(2)]
        s1, on = v3(ar(HM1, 1024), 2), v3(ar(HM1 + 1024, 1024), 2)
        ktail, ST, qin = v3(ar(SQO, 512), 2), v3(ar(SQO + 512, 256), 2), v3(ar(SQO + 768, 256), 2)
        vdec, kdec, STd = ar(SQO + 1024, 512), ar(SQO + 1536, 256), ar(SQO + 1792, 128)
        rot = ar(SQO + 1920, 288)
        th = [ar(MSO + 288 * i, T) for i in range(2)]
        bn6, mv, gv = small[:, 36:48], small[:, 48:52], small[:, 52:54]
        ms, rstd = small, None
        nrm = ar(MSO, 576)
        ms, rstd = nrm[:, 0:288], nrm[:, 288:576]
        ro = [PHO]

        def rt(n, dt=F32):
            x = ar(ro[0], n)
            ro[0] += n
            return x if dt == F32 else x.bitcast(dt)

        rl = v3(rt(108), 3)
        lgp, gm8, em8, e8 = (v3(rt(24), 3) for _ in range(4))
        gi8, ei8 = (v3(rt(24, U32), 3) for _ in range(2))
        g4 = v3(rt(12), 3)
        gf, ng, ne, gs, es, fr = (rt(3) for _ in range(6))
        pen = v3(rt(12), 3)
        lem = rt(96).rearrange("p (b g e) -> p b g e", b=3, g=NG)
        ef, pe2, idxf = (v3(rt(6), 3) for _ in range(3))
        oh = rt(192).rearrange("p (b k e) -> p b k e", b=3, k=2)
        prod = rt(192).rearrange("p (b k e) -> p b k e", b=3, k=2)
        M, Gx = v3(rt(96), 3), v3(rt(96), 3)
        idxi = v3(rt(6, I32), 3)
        rec = rt(18, I32).rearrange("p (b k r) -> p b k r", b=3, k=2)
        rec_gate = rec.bitcast(F32)[:, :, :, 2]
        cmx, cgt, npf = rt(1), rt(4), rt(1)
        Lt_ = rt(3 * PAIRS + 6, I32)
        wr_sb = rt(288)
        tok_i = [small[:, 64 + u:65 + u].bitcast(I32) for u in range(2)]
        pair_i = [small[:, 66 + u:67 + u].bitcast(I32) for u in range(2)]
        gate_c = [small[:, 68 + u:69 + u] for u in range(2)]
        npass = small[:, 60:62].bitcast(I32)
        flag = [[small[:, 74 + 6 * l + i:75 + 6 * l + i] for i in range(6)] for l in range(2)]
        assert ro[0] <= QMO
        htok = [ar(CATO + 1024 * i, 1024) for i in range(3)]
        xg = [ar(KTO + 1024 * i, 1024) for i in range(2)]
        xgT = [v3(ar(VO + 1024 * i, 1024), 8) for i in range(2)]
        yo = [ar(CATO + 3072 + 1024 * i, 1024) for i in range(2)]
        act_ = [ar(CATO + 5120 + 256 * i, 256) for i in range(2)]
        actT = [v3(ar(CATO + 5632 + 256 * i, 256), 2) for i in range(2)]
        tg = [ar(CATO + 6144 + 256 * i, 256) for i in range(2)]
        yl = [ar(CATO + 2048 * i, 2048) for i in range(3)]

        def slot(s):
            return ring[:, s * SLOT:(s + 1) * SLOT]

        def part(name):
            seq, off, tag = (SEQ_A, OFF_A, "A") if name in SEQ_A else (SEQ_B, OFF_B, "B")
            n = seq.index(name)
            return tag, n, (n + off) % R

        def uses_before(tag, s):
            return 0 if tag == "A" else sum((n + OFF_A) % R == s for n in range(len(SEQ_A)))

        def landed(eng, name):
            tag, n, s = part(name)
            eng.wait_ge(S(f"landed{s}"), 16 * (n // R + 1 + uses_before(tag, s)))
            return slot(s)

        def chain(eng, key, ins):
            counts[key] = counts.get(key, 0) + 1
            ins.then_inc(S(key), 1)
            eng.wait_ge(S(key), counts[key])

        counts = {}
        block = ctx.enter_context(nc.Block())

        NORM = {"mem": 0, "mix0": 1, "ffn0": 2, "mix1": 3, "ffn1": 4, "final": 5}
        NORM_DONE = {"mem": 16, "mix0": 24, "ffn0": 32, "mix1": 40, "ffn1": 48, "final": 56}

        def wait_used(eng, name):
            k, c = name
            sem, v = {"kv0": ("kv_sum", 2 * (c + 1)), "kv1": ("kv_sum", 8 + 2 * (c + 1)),
                      "cin": ("cin_sum", 4 * (c + 1)), "rin": ("rin_sum", 4 * (c + 1)),
                      "kc0": ("dec_scores", c + 1), "kc1": ("dec_scores", 4 + c + 1),
                      "vc0": ("dec_pv", c + 1), "vc1": ("dec_pv", 4 + c + 1),
                      "cout": ("proj", 2 * (c + 1)), "rout": ("proj", 8 + c + 1),
                      "st": (f"state_stored{c % 2}", 16 * (c // 2 + 1))}[k]
            eng.wait_ge(S(sem), v)

        @block.sync
        def _(sp):
            sp.dma_start(memT, a["memT"]).then_inc(S("mem_in"), 16)
            sp.dma_start(cst[:, :], a["cst"]).then_inc(S("const_in"), 16)
            sp.dma_start(par[:, :], a["par"]).then_inc(S("const_in"), 16)

            def source(name):
                k, c = name
                if k in ("kv0", "kv1"):
                    return a["wkv"][4 * int(k[2]) + c]
                if k in ("kc0", "kc1", "vc0", "vc1"):
                    return a[k[0] + "c"][4 * int(k[2]) + c]
                return a[k][c]

            def stream(seq, tag, off, before):
                for n, name in enumerate(seq):
                    s = (n + off) % R
                    if n < R:
                        before(n)
                    else:
                        wait_used(sp, seq[n - R])
                    src = source(name)
                    sp.dma_start(slot(s)[:, 0:src.shape[1]], src).then_inc(S(f"landed{s}"), 16)
                    if tag == "A" and n == 0:
                        sp.dma_start(xT, a["xT"]).then_inc(S("x_in"), 16)

            def experts(L, off, seq):
                def body(first, i, it):
                    for j in range(R):
                        u, c = divmod(j, 3)
                        s = (off + j) % R
                        if first:
                            wait_used(sp, seq[len(seq) - R + j])
                        elif c < 2:
                            sp.wait_ge(S(f"gu_sum{L}"), 2 * it - 1 + u)
                        else:
                            sp.wait_ge(S(f"y_sum{L}"), 4 * it - 2 + 2 * u)
                        if c < 2:
                            src = a["gu"][bass.ds(4 * i + (L * NE + 2 * u + c), 1)]
                        else:
                            src = a["dn"][bass.ds(2 * i + (L * PAIRS + u), 1)]
                        sp.dma_start(slot(s), src.rearrange("a p n -> p (a n)")) \
                          .then_inc(S(f"landed_M{L}{s}"), 16)
                body(True, 0, 0)
                with sp.Fori(1, PAIRS // 2) as i:
                    body(False, i, i)
                sp.wait_ge(S(f"npass{L}"), 1)
                more = sp.value_load(npass[0:1, L:L + 1], min_val=0, max_val=PASSES - 1)
                with sp.If(more > 0):
                    with sp.Fori(0, more) as p:
                        with sp.Fori(0, PAIRS // 2) as i:
                            body(False, i, p * (PAIRS // 2) + PAIRS // 2 + i)
                return more

            stream(SEQ_A, "A", OFF_A, lambda n: None)
            more0 = experts(0, OFF_M0, SEQ_A)

            def after_experts(n):
                u, c = divmod(n, 3)
                if n == 1:
                    sp.wait_ge(S("rows_in"), 48)
                if c < 2:
                    sp.wait_ge(S("gu_sum0"), more0 * PAIRS + (PAIRS - 1 + u))
                else:
                    sp.wait_ge(S("y_sum0"), more0 * (2 * PAIRS) + (2 * PAIRS - 2 + 2 * u))

            stream(SEQ_B, "B", OFF_B, after_experts)
            experts(1, OFF_M1, SEQ_B)

        @block.tensor
        def _(pe):
            def norm_sum(name, n):
                for k in range(KD):
                    pe.wait_ge(S("squared"), KD * NORM[name] + k + 1)
                    mm = pe.matmul(bank[7][:, 0:n], C("ones"), sq[:, k, 0:n], start=(k == 0), stop=(k == KD - 1))
                mm.then_inc(S("sumsq"), 1)

            KV_BANKS = ((0, 1, 2, 3, 4, 5, 6, 7), (4, 7, 0, 1, 2, 3, 4, 7))
            KT_BANKS = ((0, 1, 2, 3), (4, 5, 6, 0))

            def memory_kv(i, j):
                c, mb = divmod(j, 2)
                src = (hm0, hm1)[i]
                w = v3(landed(pe, (f"kv{i}", c)), KD)
                for k in range(KD):
                    if i == 0 and j == 0:
                        pe.wait_ge(S("normed"), k + 1)
                    mm = pe.matmul(bank[KV_BANKS[i][j]][:, :], src[:, k, mb * P:(mb + 1) * P], w[:, k, :],
                                   start=(k == 0), stop=(k == KD - 1))
                mm.then_inc(S("kv_sum"), 1)

            def turn_keys(i):
                for g in range(4):
                    for hd in range(2):
                        for mb in range(2):
                            mm = pe.transpose(bank[KT_BANKS[i][g]][:, hd * 256 + mb * P:hd * 256 + (mb + 1) * P],
                                              Ktok[:, mb, (2 * g + hd) * P:(2 * g + hd + 1) * P], C("ident"))
                    mm.then_inc(S("kt_turned"), 1)

            def attention(i, xo):
                pe.wait_ge(S("qmask_x"), i + 1)
                for c in range(4):
                    k2 = landed(pe, (f"kc{i}", c)).rearrange("p (b h m) -> p b h m", b=2, h=8)
                    for bi in range(2):
                        for dt in range(2):
                            for h in range(H):
                                b = 2 * c + bi
                                mm = pe.matmul(bank[0][32 * h:32 * h + 32, 0:NM],
                                               qm[:, 2 * h + dt, 32 * b:32 * b + 32], k2[:, bi, 2 * h + dt, :],
                                               start=(b == 0 and dt == 0), stop=(b == NB - 1 and dt == 1),
                                               skip_group_check=True)
                    mm.then_inc(S("dec_scores"), 1)
                jobs = [None] + [(h, tb) for h in range(H) for tb in range(2)]

                def scores(j):
                    h, tb = jobs[j]
                    if j > 2:
                        pe.wait_ge(S("exp_done"), 9 * i + j - 1)
                    for dt in range(2):
                        mm = pe.matmul(bank[1 + (j - 1) % 2][:, 0:NM], qx[:, 2 * h + dt, tb * P:(tb + 1) * P],
                                       KT[:, 2 * h + dt, :], start=(dt == 0), stop=(dt == 1))
                    mm.then_inc(S("pr_scores"), 1)

                def turn(j):
                    pe.wait_ge(S("p_ready"), 9 * i + j + 1)
                    if j == 2:
                        pe.wait_ge(S("pt0_out"), i + 1)
                    if j > 2:
                        pe.wait_ge(S("pt_out"), 8 * i + j - 2)
                    for mb in range(2):
                        mm = pe.transpose(bank[3 + j % 2][:, mb * P:(mb + 1) * P], Pm[j % 2][:, mb * P:(mb + 1) * P],
                                          C("ident"))
                    mm.then_inc(S("p_turned"), 1)

                def pv(h):
                    pe.wait_ge(S("pt_out"), 8 * i + 2 * h + 2)
                    if h >= 2:
                        pe.wait_ge(S("pv_out"), 4 * i + h - 1)
                    for dt in range(2):
                        for mb in range(2):
                            mm = pe.matmul(bank[5 + h % 2][:, dt * TP:(dt + 1) * TP],
                                           V[:, mb, (2 * h + dt) * P:(2 * h + dt + 1) * P], PT[h % 2][:, mb, :],
                                           start=(mb == 0), stop=(mb == 1))
                    mm.then_inc(S("pv_sum"), 1)

                if i:
                    pe.wait_ge(S("values_back"), 16)
                scores(1)
                scores(2)
                for j in range(9):
                    turn(j)
                    if j + 3 <= 8:
                        scores(j + 3)
                    if j >= 3 and j % 2 == 1:
                        pv((j - 3) // 2)
                pv(3)
                for c in range(4):
                    v2 = landed(pe, (f"vc{i}", c)).rearrange("p (b q n) -> p b q n", b=2, q=2)
                    if c == 0:
                        pe.wait_ge(S("pt0_out"), i + 1)
                    for bi in range(2):
                        for mb in range(2):
                            for h in range(H):
                                b = 2 * c + bi
                                mm = pe.matmul(bank[7][32 * h:32 * h + 32, 0:NM],
                                               qm[:, 4 * mb + h, 32 * b:32 * b + 32],
                                               v2[:, bi, mb, h * 256:(h + 1) * 256],
                                               start=(b == 0 and mb == 0), stop=(b == NB - 1 and mb == 1),
                                               skip_group_check=True)
                    mm.then_inc(S("dec_pv"), 1)
                pe.wait_ge(S("od_out"), i + 1)
                for dt in range(2):
                    mm = pe.transpose(bank[0][:, dt * P:(dt + 1) * P], od[:, dt * P:(dt + 1) * P], C("ident"))
                mm.then_inc(S("od_turned"), 1)

            def project_out(i, kt):
                name, per = (("cout", 2), ("rout", 1))[i]
                for o in range(KD):
                    w = v3(landed(pe, (name, o // per))[:, (o % per) * kt * P:(o % per + 1) * kt * P], kt)
                    if o == 0:
                        pe.wait_ge(S("cat_ready"), i + 1)
                    if o >= 4:
                        pe.wait_ge(S("res_add"), 8 * i + o - 3)
                    for k in range(kt):
                        mm = pe.matmul(bank[1 + o % 4][:, 0:T], w[:, k, :], cat[:, k, :],
                                       start=(k == 0), stop=(k == kt - 1))
                    mm.then_inc(S("proj"), 1)

            def route(i):
                pe.wait_ge(S("normed"), NORM_DONE[f"ffn{i}"])
                pe.wait_ge(S("router_in"), 16 * (i + 1))
                wr = v3(wr_sb, KD)
                for b, (t0, n) in enumerate(BLK):
                    for k in range(KD):
                        mm = pe.matmul(bank[6][0:n, b * 36:b * 36 + 36], hT[:, k, t0:t0 + n], wr[:, k, :],
                                       start=(k == 0), stop=(k == KD - 1))
                mm.then_inc(S("logits"), 1)
                for j in range(6):
                    b, half = divmod(j, 2)
                    t0, n = BLK[b]
                    if j >= 4:
                        pe.wait_ge(S("htok_out"), 6 * i + j - 3)
                    for k in range(4):
                        mm = pe.transpose(bank[j % 4][0:n, k * P:(k + 1) * P], hT[:, 4 * half + k, t0:t0 + n],
                                          C("ident"))
                    mm.then_inc(S("h_turned"), 1)
                if i == 0:
                    memory_kv(1, 0)
                pe.wait_ge(S("chosen"), i + 1)
                for b in range(3):
                    for bb in range(b + 1):
                        mm = pe.matmul(bank[5][:, b * NE:(b + 1) * NE], C("tri") if bb == b else C("ones"),
                                       M[:, bb, :], start=(bb == 0), stop=(bb == b))
                for bb in range(3):
                    mm = pe.matmul(bank[5][:, 3 * NE:4 * NE], C("ones"), M[:, bb, :], start=(bb == 0), stop=(bb == 2))
                mm.then_inc(S("ranks"), 1)
                if i == 0:
                    memory_kv(1, 1)
                pe.wait_ge(S("htok_out"), 6 * (i + 1))
                if i == 0:
                    for j in range(2, 8):
                        if j >= 6:
                            pe.wait_ge(S("kv1_out"), j - 5)
                        memory_kv(1, j)
                    pe.wait_ge(S("kv1_out"), 8)

            def experts(L, off):
                pe.wait_ge(S(f"npass{L}"), 1)
                npr = pe.value_load(npass[0:1, L:L + 1], min_val=0, max_val=PASSES - 1) + 1
                with pe.Fori(0, npr) as p:
                    with pe.Fori(0, PAIRS // 2) as i:
                        it = p * (PAIRS // 2) + i
                        for u in range(2):
                            g = 2 * it + u
                            pe.wait_ge(S(f"gathered{L}{u}"), 16 * (it + p) + 16)
                            for k in range(KD):
                                mm = pe.transpose(bank[k // 4][:, (k % 4) * P:(k % 4 + 1) * P],
                                                  xg[u][:, k * P:(k + 1) * P], C("ident"))
                                if k % 4 == 3:
                                    mm.then_inc(S(f"x_turned{L}"), 1)
                            w = []
                            for c in range(2):
                                s = (off + 3 * u + c) % R
                                pe.wait_ge(S(f"landed_M{L}{s}"), 16 * it + 16)
                                w.append(v3(slot(s), KD))
                            pe.wait_ge(S(f"xt_out_a{L}"), g + 1)
                            pe.wait_ge(S(f"xt_out_d{L}"), g + 1)
                            for k in range(KD):
                                for c in range(2):
                                    mm = pe.matmul(bank[2 + u][64 * c:64 * c + 64, :], xgT[u][:, k, 64 * c:64 * c + 64],
                                                   w[c][:, k, :], start=(k == 0), stop=(k == KD - 1),
                                                   skip_group_check=True)
                            mm.then_inc(S(f"gu_sum{L}"), 1)
                            pe.wait_ge(S(f"act_ready{L}"), g + 1)
                            for f in range(2):
                                mm = pe.transpose(bank[4][:, f * P:(f + 1) * P], act_[u][:, f * P:(f + 1) * P], C("ident"))
                            mm.then_inc(S(f"act_turned{L}"), 1)
                            s = (off + 3 * u + 2) % R
                            pe.wait_ge(S(f"landed_M{L}{s}"), 16 * it + 16)
                            wd = slot(s).rearrange("p (c f n) -> p c f n", c=2, f=2)
                            pe.wait_ge(S(f"actT_out{L}"), g + 1)
                            pe.wait_ge(S(f"y_out_a{L}"), g + 1)
                            pe.wait_ge(S(f"y_out_d{L}"), g + 1)
                            for n in range(2):
                                for f in range(2):
                                    for c in range(2):
                                        mm = pe.matmul(bank[5 + n][64 * c:64 * c + 64, :],
                                                       actT[u][:, f, 64 * c:64 * c + 64],
                                                       wd[:, c, f, n * 512:(n + 1) * 512],
                                                       start=(f == 0), stop=(f == 1), skip_group_check=True)
                                mm.then_inc(S(f"y_sum{L}"), 1)
                pe.wait_ge(S(f"y_out_a{L}"), npr * PAIRS + 1)
                pe.wait_ge(S(f"y_out_d{L}"), npr * PAIRS + 1)

            def combine(L):
                for j in range(6):
                    b, half = divmod(j, 2)
                    n = BLK[b][1]
                    pe.wait_ge(S("rows_added"), 3 * L + b + 1)
                    if j >= 4:
                        pe.wait_ge(S("moe_add"), 6 * L + j - 3)
                    for k in range(4):
                        mm = pe.transpose(bank[j % 4][:, k * P:k * P + n],
                                          yl[b][0:n, (4 * half + k) * P:(4 * half + k + 1) * P], C("ident", n)[:, 0:n])
                    mm.then_inc(S("rows_turned"), 1)

            def project_in(name, c, src, drained):
                w = landed(pe, (name, c)).rearrange("p (o k n) -> p o k n", o=4, k=KD)
                drained(c)
                for o in range(4):
                    for k in range(KD):
                        mm = pe.matmul(bank[4 * (c % 2) + o][:, 0:T], w[:, o, k, :], src[:, k, :],
                                       start=(k == 0), stop=(k == KD - 1))
                    mm.then_inc(S(name + "_sum"), 1)

            pe.wait_ge(S("const_in"), 32)
            norm_sum("mem", NM)
            pe.wait_ge(S("ms_out"), 1)
            norm_sum("mix0", T)
            pe.wait_ge(S("ms_out"), 2)
            for j in range(8):
                memory_kv(0, j)
            pe.wait_ge(S("ktok_out"), 4)
            turn_keys(0)
            pe.wait_ge(S("kt_out_a"), 2)
            pe.wait_ge(S("kt_out_d"), 2)
            pe.wait_ge(S("v_out"), 4)
            pe.wait_ge(S("normed"), NORM_DONE["mix0"])

            def conv_drained(c):
                if c >= 2:
                    pe.wait_ge(S("conv_out"), c - 1)
                    pe.wait_ge(S("qx_out0"), c - 1)

            for c in range(8):
                project_in("cin", c, hT, conv_drained)
            pe.wait_ge(S("conv_out"), 8)
            pe.wait_ge(S("qx_out0"), 8)
            attention(0, 8)
            project_out(0, 16)
            norm_sum("ffn0", T)
            pe.wait_ge(S("ms_out"), 3)
            route(0)
            experts(0, OFF_M0)
            combine(0)
            norm_sum("mix1", T)
            pe.wait_ge(S("keys_back"), 16)
            turn_keys(1)
            pe.wait_ge(S("kt_out_a"), 6)
            pe.wait_ge(S("ms_out"), 4)
            pe.wait_ge(S("normed"), NORM_DONE["mix1"])

            def ret_drained(c):
                if c >= 2:
                    pe.wait_ge(S("rin_out"), c - 1)
                    pe.wait_ge(S("rin_out_a"), c - 1)

            def retention(h):
                c0 = 3 * h + 2
                pe.wait_ge(S("rin_out"), c0 + 1)
                pe.wait_ge(S("rin_out_a"), c0 + 1)
                dec = slice(TP, T)
                for c in range(2):
                    for dt in range(2):
                        mm = pe.transpose(bank[0][:, (2 * c + dt) * P:(2 * c + dt + 1) * P],
                                          kTh[:, dt, c * P:(c + 1) * P], C("ident"))
                mm.then_inc(S("r_kturn"), 1)
                for c in range(2):
                    for e in range(4):
                        mm = pe.transpose(bank[1 + c][:, e * P:(e + 1) * P], vTh[:, e, c * P:(c + 1) * P], C("ident"))
                    mm.then_inc(S("r_vturn"), 1)
                for c in range(2):
                    for dt in range(2):
                        mm = pe.matmul(bank[3][:, c * P:(c + 1) * P], kTh[:, dt, c * P:(c + 1) * P],
                                       qTh[:, dt, c * P:(c + 1) * P], start=(dt == 0), stop=(dt == 1))
                mm.then_inc(S("r_scores"), 1)
                g = slice(32 * h, 32 * h + 32)
                for dt in range(2):
                    mm = pe.matmul(bank[4][g, dt * P:(dt + 1) * P], kTh[:, dt, dec], C("ident"), start=True, stop=True,
                                   skip_group_check=True)
                for dt in range(2):
                    mm = pe.matmul(bank[4][g, 256:288], kTh[:, dt, dec], qTh[:, dt, dec], start=(dt == 0),
                                   stop=(dt == 1), skip_group_check=True)
                mm.then_inc(S("r_dec"), 1)
                for e in range(4):
                    mm = pe.matmul(bank[5][g, e * P:(e + 1) * P], vTh[:, e, dec], C("ident"), start=True, stop=True,
                                   skip_group_check=True)
                mm.then_inc(S("r_dec"), 1)
                pe.wait_ge(S("r_ktail"), h + 1)
                pe.wait_ge(S("r_vtok"), 2 * h + 2)
                for dt in range(2):
                    mm = pe.matmul(bank[6 + dt][:, :], ktail[:, 0, dt * P:(dt + 1) * P], vtok[:, 0, :],
                                   start=True, stop=True)
                    mm.then_inc(S("r_s1"), 1)
                pe.wait_ge(S("r_st"), h + 1)
                pe.matmul(bank[0][:, :], ST[:, 0, :], vtok[:, 0, :], start=True, stop=True).then_inc(S("r_o"), 1)
                pe.matmul(bank[1][:, :], ST[:, 1, :], vtok[:, 1, :], start=True, stop=False)
                pe.wait_ge(S("r_s1out"), 2 * h + 2)
                for dt in range(2):
                    mm = pe.matmul(bank[1][:, :], qin[:, dt, :], s1[:, dt, :], start=False, stop=(dt == 1))
                mm.then_inc(S("r_o"), 1)
                for dt in range(2):
                    mm = pe.matmul(bank[6 + dt][:, :], ktail[:, 1, dt * P:(dt + 1) * P], vtok[:, 1, :],
                                   start=True, stop=True)
                    mm.then_inc(S("r_s2"), 1)
                for c in range(2):
                    pe.wait_ge(S("r_normed"), 2 * h + c + 1)
                    for e in range(4):
                        mm = pe.transpose(bank[2 + c][:, e * P:(e + 1) * P], on[:, c, e * P:(e + 1) * P], C("ident"))
                    mm.then_inc(S("r_oturn"), 1)
                pe.wait_ge(S("r_head"), h + 1)
                pe.wait_ge(S("r_decout_a"), h + 1)

            for c in range(14):
                project_in("rin", c, hT, ret_drained)
                if c % 3 == 2:
                    retention(c // 3)
            pe.wait_ge(S("rin_out"), 14)
            pe.wait_ge(S("rin_out_a"), 14)
            pe.matmul(bank[0][:, :], STd, vdec, start=True, stop=False, skip_group_check=True)
            pe.wait_ge(S("qmask_r"), 4)
            for b in range(NB):
                st = landed(pe, ("st", b)).rearrange("p (h n) -> p h n", h=8)
                for dt in range(2):
                    for h in range(H):
                        mm = pe.matmul(bank[0][32 * h:32 * h + 32, :], qm[:, 2 * h + dt, 32 * b:32 * b + 32],
                                       st[:, 2 * h + dt, :], start=False, stop=(b == NB - 1 and dt == 1),
                                       skip_group_check=True)
                mm.then_inc(S("d_cross"), 1)
                for h in range(H):
                    n = b * H + h
                    pe.wait_ge(S("kvar_ready"), n + 1)
                    for dt in range(2):
                        q = 2 * n + dt
                        if q >= 4:
                            pe.wait_ge(S("d_state"), q - 3)
                        mm = pe.matmul(bank[1 + q % 4][:, :], kvar[n % 2][:, dt * P:(dt + 1) * P], vdec,
                                       start=True, stop=True)
                        mm.then_inc(S("d_add"), 1)
            pe.wait_ge(S("r_normed"), 9)
            pe.wait_ge(S("d_state"), 64)
            for e in range(4):
                mm = pe.transpose(bank[2][:, e * P:(e + 1) * P], on[:, 0, e * P:(e + 1) * P], C("ident"))
            mm.then_inc(S("r_oturn"), 1)
            pe.wait_ge(S("d_out"), 1)
            attention(1, 16)
            project_out(1, 24)
            norm_sum("ffn1", T)
            pe.wait_ge(S("ms_out"), 5)
            route(1)
            experts(1, OFF_M1)
            combine(1)
            norm_sum("final", T)

        @block.scalar
        def _(act):
            def squares(name, src, n, ready):
                if NORM[name]:
                    act.wait_ge(S("sumsq"), NORM[name])
                ready()
                for k in range(KD):
                    act.activation(sq[:, k, 0:n], src[:, k, :], ACT.Square).then_inc(S("squared"), 1)
                act.wait_ge(S("sumsq"), NORM[name] + 1)
                if NORM[name]:
                    act.wait_ge(S("normed"), NORM_DONE[name] - (16 if name == "mem" else 8))
                act.activation(ms[:, 0:n], bank[7][:, 0:n], ACT.Sqrt, scale=1.0 / D, bias=C("eps")) \
                   .then_inc(S("ms_out"), 1)

            def memory_kv():
                for j in range(4):
                    act.wait_ge(S("kv_sum"), j + 1)
                    act.activation(Ktok[:, j % 2, (j // 2) * 512:(j // 2 + 1) * 512], bank[j][:, :], ACT.Copy) \
                       .then_inc(S("ktok_out"), 1)
                for g in (1, 3):
                    act.wait_ge(S("kt_turned"), g + 1)
                    act.activation(KT[:, 2 * g:2 * g + 2, :], v3(bank[g][:, :], 2), ACT.Copy) \
                       .then_inc(S("kt_out_a"), 1)

            def memory_kv_ahead():
                for j in range(8):
                    act.wait_ge(S("kv_sum"), 8 + j + 1)
                    dst = (keys1, values1)[j // 4][:, j % 2, (j // 2 % 2) * 512:(j // 2 % 2 + 1) * 512]
                    act.activation(dst, bank[(4, 7, 0, 1, 2, 3, 4, 7)[j]][:, :], ACT.Copy).then_inc(S("kv1_out"), 1)
                    if j % 4 == 3:
                        act.wait_ge(S("kv1_out"), j + 1)
                        out, src, sem = ((a["out_mk"], keys1, "keys_stored1"), (a["out_mv"], values1, "values_stored1"))[j // 4]
                        act.dma_start(out[1].rearrange("(m p) n -> p m n", p=P), src).then_inc(S(sem), 16)

            def keys_turned():
                for g in range(4):
                    act.wait_ge(S("kt_turned"), 4 + g + 1)
                    act.activation(KT[:, 2 * g:2 * g + 2, :], v3(bank[(4, 5, 6, 0)[g]][:, :], 2), ACT.Copy) \
                       .then_inc(S("kt_out_a"), 1)

            def attention(i):
                act.wait_ge(S("normed"), NORM_DONE[f"mix{i}"])
                for j in range(9):
                    act.wait_ge(S("neg_max"), 9 * i + j + 1)
                    if j >= 2:
                        act.wait_ge(S("p_turned"), 9 * i + j - 1)
                    src = bank[0] if j == 0 else bank[1 + (j - 1) % 2]
                    act.activation(Pm[j % 2], src[:, 0:NM], ACT.Exp, bias=nb_[:, j:j + 1], scale=1.0 / 16,
                                   accum_out=rs[:, j:j + 1]).then_inc(S("exp_done"), 1)
                    if j >= 2:
                        turned(i, j - 1)
                turned(i, 8)
                act.wait_ge(S("dec_pv"), 4 * i + 4)
                act.activation(od, bank[7][:, 0:NM], ACT.Copy).then_inc(S("od_out"), 1)

            def turned(i, j):
                h, tb = divmod(j - 1, 2)
                act.wait_ge(S("p_turned"), 9 * i + j + 1)
                if h >= 2:
                    act.wait_ge(S("pv_sum"), 4 * i + h - 1)
                act.activation(PT[h % 2][:, :, tb * P:(tb + 1) * P], v3(bank[3 + j % 2][:, 0:256], 2), ACT.Copy) \
                   .then_inc(S("pt_out"), 1)

            def route(i):
                for j in range(6):
                    b, half = divmod(j, 2)
                    n = BLK[b][1]
                    act.wait_ge(S("h_turned"), 6 * i + j + 1)
                    act.activation(htok[b][0:n, half * 512:(half + 1) * 512], bank[j % 4][0:n, :], ACT.Copy) \
                       .then_inc(S("htok_out"), 1)
                act.activation(small[:, 72:73], C("eps"), ACT.Copy).then_inc(S(f"y_out_a{i}"), 1)
                act.wait_ge(S("g_max"), i + 1)
                for b in range(3):
                    act.activation(g4[:, b, :], rl[:, b, 0:NG], ACT.Exp, bias=ng[:, b:b + 1],
                                   accum_out=gs[:, b:b + 1]).then_inc(S("g_exp"), 1)
                act.wait_ge(S("e_max"), i + 1)
                for b in range(3):
                    act.activation(e8[:, b, :], em8[:, b, :], ACT.Exp, bias=ne[:, b:b + 1],
                                   accum_out=es[:, b:b + 1]).then_inc(S("e_exp"), 1)

            def experts(L):
                act.wait_ge(S(f"npass{L}"), 1)
                npr = act.value_load(npass[0:1, L:L + 1], min_val=0, max_val=PASSES - 1) + 1
                with act.Fori(0, npr) as p:
                    with act.Fori(0, PAIRS // 2) as i:
                        it = p * (PAIRS // 2) + i
                        for u in range(2):
                            g = 2 * it + u
                            act.wait_ge(S(f"x_turned{L}"), 2 * g + 1)
                            act.activation(xgT[u][:, 0:4, :], v3(bank[0][:, :], 4), ACT.Copy) \
                               .then_inc(S(f"xt_out_a{L}"), 1)
                            act.wait_ge(S(f"gu_sum{L}"), g + 1)
                            act.activation(tg[u], bank[2 + u][:, 0:FF], ACT.Tanh, scale=0.5) \
                               .then_inc(S(f"tanh{L}"), 1)
                            act.wait_ge(S(f"y_sum{L}"), 2 * g + 1)
                            act.wait_ge(S(f"scattered{L}"), 16 * g + 16)
                            act.activation(yo[u][:, 0:512], bank[5][:, :], ACT.Copy).then_inc(S(f"y_out_a{L}"), 1)

            act.wait_ge(S("const_in"), 32)
            act.wait_ge(S("mem_in"), 16)
            squares("mem", memT, NM, lambda: None)
            act.wait_ge(S("x_in"), 16)
            squares("mix0", xT, T, lambda: None)
            memory_kv()
            for c in range(8):
                act.wait_ge(S("cin_sum"), 4 * c + 1)
                if c >= 2:
                    act.wait_ge(S("conv_out"), c - 1)
                act.activation(c_sb[c % 2], bank[4 * (c % 2)][:, 0:T], ACT.Copy).then_inc(S("c_out"), 1)
                act.wait_ge(S("cin_sum"), 4 * c + 4)
                if c == 0:
                    act.wait_ge(S("keys_stored0"), 16)
                act.activation(qx[:, c, :], bank[4 * (c % 2) + 3][:, 0:T], ACT.Copy).then_inc(S("qx_out0"), 1)
            attention(0)
            squares("ffn0", xT, T, lambda: act.wait_ge(S("res_add"), 8))
            route(0)
            memory_kv_ahead()
            experts(0)
            act.wait_ge(S("values_stored1"), 16)
            squares("mix1", xT, T, lambda: act.wait_ge(S("moe_add"), 6))
            keys_turned()
            for c in range(12):
                kind, h = c % 3, c // 3
                for o in range(4):
                    act.wait_ge(S("rin_sum"), 4 * c + o + 1)
                    bk = bank[4 * (c % 2) + o][:, 0:T]
                    if kind == 1:
                        ins = act.activation(vTh[:, o, :], bk, ACT.Copy)
                    elif kind == 2:
                        if 4 * h + o >= 2:
                            act.wait_ge(S("r_gate"), 4 * h + o - 1)
                        act.activation(th[o % 2], bk, ACT.Tanh, scale=0.5).then_inc(S("r_tanh"), 1)
                        ins = act.activation(cat[:, 4 * h + o, :], bk, ACT.Copy,
                                             scale=G("gn")[:, 4 * h + o:4 * h + o + 1])
                        if o < 3:
                            ins.then_inc(S("r_gg"), 1)
                if kind == 0:
                    act.nop().then_inc(S("rin_out_a"), 1)
                elif kind == 1:
                    ins.then_inc(S("rin_out_a"), 1)
                else:
                    ins.then_inc(S("r_gg"), 1)
                    act.wait_ge(S("r_gg"), 4 * h + 4)
                    act.nop().then_inc(S("rin_out_a"), 1)
                    for q in range(2):
                        act.wait_ge(S("r_vturn"), 2 * h + q + 1)
                        act.activation(vtok[:, q, :], bank[1 + q][:, :], ACT.Copy).then_inc(S("r_vtok"), 1)
                    g = slice(32 * h, 32 * h + 32)
                    act.wait_ge(S("r_dec"), 2 * h + 2)
                    act.activation(vdec[g, :], bank[5][g, :], ACT.Copy).then_inc(S("r_decout_a"), 1)
                    for dt in range(2):
                        act.wait_ge(S("r_s1"), 2 * h + dt + 1)
                        if h and dt == 0:
                            act.wait_ge(S("ret_stored"), 16 * h)
                        act.activation(s1[:, dt, :], bank[6 + dt][:, :], ACT.Copy).then_inc(S("r_s1out"), 1)
            for c in (12, 13):
                for o in range(4):
                    act.wait_ge(S("rin_sum"), 4 * c + o + 1)
                    ins = act.activation(qx[:, 4 * (c - 12) + o, :], bank[4 * (c % 2) + o][:, 0:T], ACT.Copy)
                ins.then_inc(S("rin_out_a"), 1)
            attention(1)
            squares("ffn1", xT, T, lambda: act.wait_ge(S("res_add"), 16))
            route(1)
            experts(1)
            squares("final", xT, T, lambda: act.wait_ge(S("moe_add"), 12))

        @block.vector
        def _(dve):
            def V_(ins):
                chain(dve, "vector_chain", ins)

            def norm(name, src, dests, n, wait_dest=None):
                dve.wait_ge(S("ms_out"), NORM[name] + 1)
                V_(dve.reciprocal(rstd[:, 0:n], ms[:, 0:n]))
                for dst, gname in dests:
                    for k in range(KD):
                        dve.scalar_tensor_tensor(out=dst[:, k, :], in0=src[:, k, :], scalar=G(gname)[:, k:k + 1],
                                                 in1=rstd[:, 0:n], op0=ALU.mult, op1=ALU.mult) \
                           .then_inc(S("normed"), 1)

            def memory_kv():
                for j in range(4, 8):
                    dve.wait_ge(S("kv_sum"), j + 1)
                    dve.tensor_copy(V[:, j % 2, (j // 2 - 2) * 512:(j // 2 - 1) * 512], bank[j][:, :]) \
                       .then_inc(S("v_out"), 1)
                for g in (0, 2):
                    dve.wait_ge(S("kt_turned"), g + 1)
                    dve.tensor_copy(KT[:, 2 * g:2 * g + 2, :], v3(bank[g][:, :], 2)).then_inc(S("kt_out_d"), 1)

            def attention(i, xo):
                qd = qx[:, :, TP:T].rearrange("p h (b s) -> p h b s", s=NS)
                dve.tensor_copy(qm_diag, qd).then_inc(S("qmask_x"), 1)

                def maximum(j):
                    if j == 0:
                        dve.wait_ge(S("dec_scores"), 4 * i + 4)
                    else:
                        dve.wait_ge(S("pr_scores"), 8 * i + j)
                    src = bank[0] if j == 0 else bank[1 + (j - 1) % 2]
                    V_(dve.tensor_reduce(mx[:, j:j + 1], src[:, 0:NM], AX.X, ALU.max))
                    dve.tensor_scalar(nb_[:, j:j + 1], mx[:, j:j + 1], -1.0 / 16, None, ALU.mult) \
                       .then_inc(S("neg_max"), 1)

                def normalise(j):
                    dve.wait_ge(S("exp_done"), 9 * i + j + 1)
                    V_(dve.reciprocal(rr[:, j:j + 1], rs[:, j:j + 1]))
                    dve.tensor_scalar(Pm[j % 2], Pm[j % 2], rr[:, j:j + 1], None, ALU.mult).then_inc(S("p_ready"), 1)

                def pv_out(h):
                    dve.wait_ge(S("pv_sum"), 4 * i + h + 1)
                    dve.tensor_copy(cat[:, xo + 2 * h:xo + 2 * h + 2, 0:TP], v3(bank[5 + h % 2][:, :], 2)) \
                       .then_inc(S("pv_out"), 1)

                maximum(0)
                for j in range(9):
                    if j + 1 < 9:
                        maximum(j + 1)
                    normalise(j)
                    if j == 0:
                        dve.wait_ge(S("p_turned"), 9 * i + 1)
                        for mb in range(2):
                            ins = dve.tensor_copy(qm_diag[:, 4 * mb:4 * mb + 4],
                                                  bank[3][:, mb * P:(mb + 1) * P]
                                                  .rearrange("p (h b s) -> p h b s", h=H, b=NB))
                            if mb == 0:
                                V_(ins)
                        ins.then_inc(S("pt0_out"), 1)
                    if j >= 6 and j % 2 == 0:
                        pv_out((j - 6) // 2)
                pv_out(2)
                pv_out(3)
                dve.wait_ge(S("od_turned"), i + 1)
                for dt in range(2):
                    ins = dve.tensor_copy(cat[:, xo:xo + 8, TP:T].rearrange("p (h d) t -> p h d t", d=2)[:, :, dt, :],
                                          bank[0][:, dt * P:(dt + 1) * P].rearrange("p (h t) -> p h t", h=H))
                    if dt == 0:
                        V_(ins)
                ins.then_inc(S("cat_out"), 1)
                dve.wait_ge(S("cat_out"), i + 1)
                dve.wait_ge(S("pv_out"), 4 * i + 4)
                dve.nop().then_inc(S("cat_ready"), 1)

            def residual(i):
                for o in range(KD):
                    dve.wait_ge(S("proj"), 8 * i + o + 1)
                    dve.tensor_tensor(xT[:, o, :], xT[:, o, :], bank[1 + o % 4][:, 0:T], ALU.add) \
                       .then_inc(S("res_add"), 1)

            def route(i):
                V_(dve.memset(rl, 0.0))
                V_(dve.memset(lgp, -BIG))
                dve.wait_ge(S("logits"), i + 1)
                V_(dve.tensor_copy(rl[:, 0:2, :], v3(bank[6][:, 0:72], 2)))
                V_(dve.tensor_copy(rl[0:32, 2, :], bank[6][0:32, 72:108]))
                V_(dve.tensor_copy(lgp[:, :, 0:NG], rl[:, :, 0:NG]))
                for b in range(3):
                    V_(dve.max(gm8[:, b, :], lgp[:, b, :]))
                    V_(dve.max_index(gi8[:, b, :], gm8[:, b, :], lgp[:, b, :]))
                dve.tensor_scalar(ng, gm8[:, :, 0], -1.0, None, ALU.mult).then_inc(S("g_max"), 1)
                V_(dve.tensor_copy(gf, gi8[:, :, 0]))
                V_(dve.tensor_tensor(pen, C("iota")[:, 0:NG].unsqueeze(1).to_broadcast([P, 3, NG]),
                                     gf.unsqueeze(2).to_broadcast([P, 3, NG]), ALU.is_equal))
                V_(dve.tensor_scalar(pen, pen, -1.0, BIG, ALU.add, ALU.mult))
                for b in range(3):
                    V_(dve.tensor_tensor(lem[:, b], rl[:, b, NG:].rearrange("p (g e) -> p g e", g=NG),
                                         pen[:, b, :].unsqueeze(2).to_broadcast([P, NG, EPG]), ALU.add))
                lemf = lem.rearrange("p b g e -> p b (g e)")
                for b in range(3):
                    V_(dve.max(em8[:, b, :], lemf[:, b, :]))
                    V_(dve.max_index(ei8[:, b, :], em8[:, b, :], lemf[:, b, :]))
                dve.tensor_scalar(ne, em8[:, :, 0], -1.0, None, ALU.mult).then_inc(S("e_max"), 1)
                V_(dve.tensor_copy(ef, ei8[:, :, 0:2]))
                for k in range(2):
                    V_(dve.tensor_tensor(oh[:, :, k, :], C("iota").unsqueeze(1).to_broadcast([P, 3, NE]),
                                         ef[:, :, k].unsqueeze(2).to_broadcast([P, 3, NE]), ALU.is_equal))
                V_(dve.tensor_tensor(M, oh[:, :, 0, :], oh[:, :, 1, :], ALU.add))
                dve.tensor_tensor(M, M, C("valid").unsqueeze(2).to_broadcast([P, 3, NE]), ALU.mult) \
                   .then_inc(S("chosen"), 1)
                dve.wait_ge(S("e_exp"), 3 * i + 3)
                dve.wait_ge(S("g_exp"), 3 * i + 3)
                V_(dve.reciprocal(es, es))
                V_(dve.tensor_tensor(pe2, e8[:, :, 0:2], es.unsqueeze(2).to_broadcast([P, 3, 2]), ALU.mult))
                V_(dve.tensor_tensor(fr, pe2[:, :, 0], pe2[:, :, 1], ALU.add))
                V_(dve.tensor_tensor(fr, fr, gs, ALU.mult))
                V_(dve.reciprocal(fr, fr))
                V_(dve.tensor_scalar(fr, fr, 0.5, None, ALU.mult))
                V_(dve.tensor_tensor(pe2, pe2, fr.unsqueeze(2).to_broadcast([P, 3, 2]), ALU.mult))
                ci = cst[:, :].bitcast(I32)
                tk, pr = CC["tok"][0], CC["pair"][0]
                V_(dve.tensor_copy(rec_gate, pe2))
                V_(dve.tensor_copy(rec[:, :, :, 0], ci[:, tk:tk + 6].rearrange("p (b k) -> p b k", b=3)))
                V_(dve.tensor_copy(rec[:, :, :, 1], ci[:, pr:pr + 6].rearrange("p (b k) -> p b k", b=3)))
                dve.wait_ge(S("ranks"), i + 1)
                dve.memset(small[:, 73:74], 0.0).then_inc(S(f"y_out_d{i}"), 1)
                V_(dve.scalar_tensor_tensor(out=Gx, in0=v3(bank[5][:, 0:96], 3), scalar=float(PAIRS),
                                            in1=C("cexp").unsqueeze(1).to_broadcast([P, 3, NE]),
                                            op0=ALU.mult, op1=ALU.add))
                for k in range(2):
                    V_(dve.tensor_tensor(prod[:, :, k, :], oh[:, :, k, :], Gx, ALU.mult))
                V_(dve.tensor_reduce(idxf, prod, AX.X, ALU.add))
                V_(dve.tensor_tensor(idxf, idxf, C("far").unsqueeze(2).to_broadcast([P, 3, 2]), ALU.add))
                dve.tensor_copy(idxi, idxf).then_inc(S("places"), 1)
                V_(dve.tensor_reduce(cmx[0:1, :], bank[5][0:1, 96:128], AX.X, ALU.max))
                V_(dve.tensor_scalar(cgt[0:1, :], C("thr")[0:1, :], cmx[0:1, 0:1], None, ALU.is_lt))
                V_(dve.tensor_reduce(npf[0:1, :], cgt[0:1, :], AX.X, ALU.add))
                dve.tensor_copy(npass[0:1, i:i + 1], npf[0:1, :]).then_inc(S(f"npass{i}"), 1)

            def experts(L):
                dve.wait_ge(S(f"npass{L}"), 1)
                npr = dve.value_load(npass[0:1, L:L + 1], min_val=0, max_val=PASSES - 1) + 1
                with dve.Fori(0, npr) as p:
                    with dve.Fori(0, PAIRS // 2) as i:
                        it = p * (PAIRS // 2) + i
                        for u in range(2):
                            g = 2 * it + u
                            dve.wait_ge(S(f"x_turned{L}"), 2 * g + 2)
                            dve.tensor_copy(xgT[u][:, 4:8, :], v3(bank[1][:, :], 4)).then_inc(S(f"xt_out_d{L}"), 1)
                            dve.wait_ge(S(f"tanh{L}"), g + 1)
                            dve.scalar_tensor_tensor(out=tg[u], in0=tg[u], scalar=1.0, in1=bank[2 + u][:, 0:FF],
                                                     op0=ALU.add, op1=ALU.mult).then_inc(S(f"silu{L}"), 1)
                            dve.wait_ge(S(f"silu{L}"), g + 1)
                            dve.scalar_tensor_tensor(out=act_[u], in0=tg[u], scalar=gate_c[u],
                                                     in1=bank[2 + u][:, FF:2 * FF], op0=ALU.mult, op1=ALU.mult) \
                               .then_inc(S(f"act_ready{L}"), 1)
                            dve.wait_ge(S(f"act_turned{L}"), g + 1)
                            dve.tensor_copy(actT[u], v3(bank[4][:, 0:256], 2)).then_inc(S(f"actT_out{L}"), 1)
                            dve.wait_ge(S(f"y_sum{L}"), 2 * g + 2)
                            dve.wait_ge(S(f"scattered{L}"), 16 * g + 16)
                            dve.tensor_copy(yo[u][:, 512:1024], bank[6][:, :]).then_inc(S(f"y_out_d{L}"), 1)

            def combine(L):
                for b, (t0, n) in enumerate(BLK):
                    dve.wait_ge(S("rows_in"), 16 * (3 * L + 3))
                    dve.tensor_tensor(yl[b][0:n, 0:D], yl[b][0:n, 0:D], yl[b][0:n, D:2 * D], ALU.add) \
                       .then_inc(S("rows_added"), 1)
                for j in range(6):
                    b, half = divmod(j, 2)
                    t0, n = BLK[b]
                    dve.wait_ge(S("rows_turned"), 6 * L + j + 1)
                    dst = xT[:, 4 * half:4 * half + 4, t0:t0 + n]
                    dve.tensor_tensor(dst, dst, v3(bank[j % 4][:, :], 4)[:, :, 0:n], ALU.add) \
                       .then_inc(S("moe_add"), 1)

            def group_norm(src, dst, ready, n):
                ready()
                V_(dve.bn_stats(bn6[:, 0:6], src[:, :]))
                V_(dve.bn_aggr(mv[:, 0:2], bn6[:, 0:6]))
                dve.tensor_scalar(mv[:, 1:2], mv[:, 1:2], EPS, None, ALU.add).then_inc(S("r_var"), 1)
                dve.wait_ge(S("r_pow"), n + 1)
                V_(dve.tensor_scalar(gv[:, 1:2], gv[:, 0:1], 0.5, None, ALU.mult))
                dve.tensor_scalar(dst, src[:, :], mv[:, 0:1], gv[:, 1:2], ALU.subtract, ALU.mult) \
                   .then_inc(S("r_normed"), 1)

            dve.wait_ge(S("const_in"), 32)
            dve.wait_ge(S("mem_in"), 16)
            norm("mem", memT, ((hm0, "mem0"), (hm1, "mem1")), NM)
            dve.wait_ge(S("x_in"), 16)
            norm("mix0", xT, ((hT, "mix0"),), T)
            memory_kv()
            V_(dve.memset(qm_, 0.0))
            for c in range(8):
                bk = [bank[4 * (c % 2) + o][:, 0:T] for o in range(4)]
                f, y = full[c % 2], yc[c % 2]
                fd = f[:, 258:306].rearrange("p (b t) -> p b t", b=NB)
                yd = y[:, TP:T].rearrange("p (b t) -> p b t", b=NB)
                if c == 0:
                    dve.wait_ge(S("states_in"), 16)
                dve.memset(f[:, 0:2], 0.0)
                dve.tensor_copy(fd[:, :, 0:2], stc[:, c, :].rearrange("p (b t) -> p b t", b=NB))
                dve.wait_ge(S("c_out"), c + 1)
                dve.wait_ge(S("cin_sum"), 4 * c + 2)
                dve.tensor_tensor(f[:, 2:258], c_sb[c % 2][:, 0:TP], bk[1][:, 0:TP], ALU.mult)
                V_(dve.tensor_tensor(fd[:, :, 2:6], c_sb[c % 2][:, TP:T].rearrange("p (b t) -> p b t", b=NB),
                                     bk[1][:, TP:T].rearrange("p (b t) -> p b t", b=NB), ALU.mult))
                w = G("cw")[:, 3 * c:3 * c + 3]
                dve.tensor_scalar(y[:, 0:TP], f[:, 0:TP], w[:, 0:1], None, ALU.mult)
                V_(dve.tensor_scalar(yd, fd[:, :, 0:4], w[:, 0:1], None, ALU.mult))
                for q in (1, 2):
                    dve.scalar_tensor_tensor(out=y[:, 0:TP], in0=f[:, q:TP + q], scalar=w[:, q:q + 1],
                                             in1=y[:, 0:TP], op0=ALU.mult, op1=ALU.add)
                    V_(dve.scalar_tensor_tensor(out=yd, in0=fd[:, :, q:q + 4], scalar=w[:, q:q + 1], in1=yd,
                                                op0=ALU.mult, op1=ALU.add))
                dve.tensor_copy(cvp[:, c, :], f[:, 256:258])
                dve.tensor_copy(cvs[:, c, :].rearrange("p (b t) -> p b t", b=NB), fd[:, :, 4:6])
                dve.wait_ge(S("cin_sum"), 4 * c + 3)
                dve.tensor_tensor(cat[:, c, :], y, bk[2], ALU.mult).then_inc(S("conv_out"), 1)
            dve.wait_ge(S("conv_out"), 8)
            dve.wait_ge(S("qx_out0"), 8)
            attention(0, 8)
            residual(0)
            norm("ffn0", xT, ((hT, "ffn0"),), T)
            route(0)
            experts(0)
            combine(0)
            dve.wait_ge(S("keys_stored1"), 16)
            norm("mix1", xT, ((hT, "mix1"),), T)
            V_(dve.memset(STd, 0.0))
            cos, sin = C("cos"), C("sin")
            for c in range(12):
                kind, h = c % 3, c // 3
                g = slice(32 * h, 32 * h + 32)
                bk = [bank[4 * (c % 2) + o][:, 0:T] for o in range(4)]
                if kind == 0:
                    for n, dst in ((0, qTh), (2, kTh)):
                        dve.wait_ge(S("rin_sum"), 4 * c + n + 2)
                        V_(dve.tensor_tensor(dst[:, 0, :], bk[n], cos, ALU.mult))
                        V_(dve.tensor_tensor(rot, bk[n + 1], sin, ALU.mult))
                        V_(dve.tensor_tensor(dst[:, 0, :], dst[:, 0, :], rot, ALU.subtract))
                        V_(dve.tensor_tensor(dst[:, 1, :], bk[n], sin, ALU.mult))
                        V_(dve.tensor_tensor(rot, bk[n + 1], cos, ALU.mult))
                        V_(dve.tensor_tensor(dst[:, 1, :], dst[:, 1, :], rot, ALU.add))
                    inner = C("inner")[:, h * P:(h + 1) * P]
                    dve.tensor_tensor(qin, qTh[:, :, P:2 * P], inner.unsqueeze(1).to_broadcast([P, 2, P]), ALU.mult)
                    for dt in range(2):
                        ins = dve.tensor_tensor(qm_diag[:, 2 * h + dt],
                                                qTh[:, dt, TP:T].rearrange("p (b s) -> p b s", s=NS),
                                                inner[:, 0:NS].unsqueeze(1).to_broadcast([P, NB, NS]), ALU.mult)
                        if dt == 0:
                            V_(ins)
                    ins.then_inc(S("qmask_r"), 1)
                    dve.wait_ge(S("qmask_r"), h + 1)
                    dve.nop().then_inc(S("rin_out"), 1)
                elif kind == 1:
                    dve.nop().then_inc(S("rin_out"), 1)
                else:
                    for o in range(4):
                        n = 4 * h + o
                        dve.wait_ge(S("r_tanh"), n + 1)
                        dve.wait_ge(S("r_gg"), n + 1)
                        ins = dve.scalar_tensor_tensor(out=cat[:, n, :], in0=th[o % 2], scalar=1.0, in1=cat[:, n, :],
                                                       op0=ALU.add, op1=ALU.mult)
                        ins.then_inc(S("r_gate"), 1)
                    dve.wait_ge(S("r_gate"), 4 * h + 4)
                    dve.nop().then_inc(S("rin_out"), 1)
                    dve.wait_ge(S("r_kturn"), h + 1)
                    dve.tensor_scalar(ktail, v3(bank[0][:, :], 2), C("tail")[:, h:h + 1], None, ALU.mult) \
                       .then_inc(S("r_ktail"), 1)
                    dve.wait_ge(S("r_scores"), h + 1)
                    dve.tensor_tensor(ST, v3(bank[3][:, 0:256], 2),
                                      C("decay")[:, h * P:(h + 1) * P].unsqueeze(1).to_broadcast([P, 2, P]),
                                      ALU.mult).then_inc(S("r_st"), 1)
                    dve.wait_ge(S("r_dec"), 2 * h + 1)
                    V_(dve.tensor_scalar(kdec[g, :], bank[4][g, 0:256], C("tdec")[g, 0:1], None, ALU.mult))
                    V_(dve.tensor_tensor(STd[g, g], bank[4][g, 256:288], C("dmask")[g, :], ALU.mult))
                    for q in range(2):
                        group_norm(bank[q], on[:, q, :], lambda: dve.wait_ge(S("r_o"), 2 * h + q + 1), 2 * h + q)
                    for dt in range(2):
                        dve.wait_ge(S("r_s2"), 2 * h + dt + 1)
                        ins = dve.scalar_tensor_tensor(out=s1[:, dt, :], in0=s1[:, dt, :],
                                                       scalar=float(np.exp(P * LOGG[h])),
                                                       in1=bank[6 + dt][:, :], op0=ALU.mult, op1=ALU.add)
                        ins.then_inc(S("r_s2out"), 1)
                    for q in range(2):
                        dve.wait_ge(S("r_oturn"), 2 * h + q + 1)
                        dst = cat[:, 4 * h:4 * h + 4, q * P:(q + 1) * P]
                        ins = dve.tensor_tensor(dst, dst, v3(bank[2 + q][:, :], 4), ALU.mult)
                        if q == 0:
                            V_(ins)
                    ins.then_inc(S("r_head"), 1)
            dve.nop().then_inc(S("rin_out"), 1)
            dve.nop().then_inc(S("rin_out"), 1)
            for b in range(NB):
                st = slot(part(("st", b))[2]).rearrange("p (h n) -> p h n", h=8)
                landed(dve, ("st", b))
                dve.wait_ge(S("d_cross"), b + 1)
                for h in range(H):
                    for dt in range(2):
                        q = 8 * b + 2 * h + dt
                        dve.wait_ge(S("d_add"), q + 1)
                        dve.scalar_tensor_tensor(out=st[:, 2 * h + dt, :], in0=st[:, 2 * h + dt, :],
                                                 scalar=float(np.exp(NS * LOGG[h])), in1=bank[1 + q % 4][:, :],
                                                 op0=ALU.mult, op1=ALU.add).then_inc(S("d_state"), 1)
            group_norm(bank[0], on[:, 0, :], lambda: None, 8)
            dve.wait_ge(S("r_oturn"), 9)
            for e in range(4):
                dst = cat[:, 0:16, TP:T].rearrange("p (h e) t -> p h e t", e=4)[:, :, e, :]
                ins = dve.tensor_tensor(dst, dst, bank[2][:, e * P:(e + 1) * P].rearrange("p (h t) -> p h t", h=H),
                                        ALU.mult)
                if e < 3:
                    V_(ins)
            ins.then_inc(S("d_out"), 1)
            dve.wait_ge(S("rin_out_a"), 14)
            attention(1, 16)
            residual(1)
            norm("ffn1", xT, ((hT, "ffn1"),), T)
            route(1)
            experts(1)
            combine(1)
            norm("final", xT, ((hT, "final"),), T)

        @block.gpsimd
        def _(pool):
            def store_state(b):
                pool.wait_ge(S("d_state"), 8 * (b + 1))
                if b >= 2:
                    pool.wait_ge(S(f"state_stored{b % 2}"), 16 * (b // 2))
                pool.dma_start(a["out_rs"][b], slot(part(("st", b))[2]).rearrange("p (h n) -> p h n", h=8)) \
                    .then_inc(S(f"state_stored{b % 2}"), 16)

            def store_memory():
                pool.wait_ge(S("ktok_out"), 4)
                pool.dma_start(a["out_mk"][0].rearrange("(m p) n -> p m n", p=P), Ktok).then_inc(S("keys_stored0"), 16)
                pool.wait_ge(S("v_out"), 4)
                pool.dma_start(a["out_mv"][0].rearrange("(m p) n -> p m n", p=P), V).then_inc(S("values_stored0"), 16)

            def memory_back():
                pool.wait_ge(S("keys_stored1"), 16)
                pool.dma_start(Ktok, a["out_mk"][1].rearrange("(m p) n -> p m n", p=P)).then_inc(S("keys_back"), 16)
                pool.wait_ge(S("values_stored1"), 16)
                pool.dma_start(V, a["out_mv"][1].rearrange("(m p) n -> p m n", p=P)).then_inc(S("values_back"), 16)

            def route(i):
                pool.wait_ge(S("cat_ready"), i + 1)
                pool.dma_start(wr_sb, a["wr"][i]).then_inc(S("router_in"), 16)
                pool.wait_ge(S(f"values_stored{i}"), 16)
                for b, (t0, n) in enumerate(BLK):
                    pool.wait_ge(S("htok_out"), 6 * i + 2 * b + 2)
                    pool.dma_start(dram_h[i][t0:t0 + n, :], htok[b][0:n, :]).then_inc(S("h_stored"), 16)
                for u in range(2):
                    pool.memset(xg[u], 0.0).then_inc(S("xg_clear"), 1)
                for u in range(2):
                    pool.dma_start(Lt_[:, 3 * (PAIRS + u):3 * (PAIRS + u) + 3], a["lfill"][:, 0:3]) \
                        .then_inc(S(f"scattered{i}"), 16)
                    pool.wait_ge(S(f"scattered{i}"), 16 * u + 16)
                pool.wait_ge(S("xg_clear"), 2 * i + 2)
                pool.wait_ge(S("places"), i + 1)
                pool.wait_ge(S("lists_filled"), 32)
                for b in range(3):
                    for k in range(2):
                        pool.indirect_dma_start(out=dram_l[i], out_offset=bass.IndirectOffsetOnAxis(
                            ap=idxi[:, b, k:k + 1].bitcast(U32), axis=0), in_=rec[:, b, k, :], in_offset=None,
                            bounds_check=2 * LROW - 1, oob_is_err=False).then_inc(S("listed"), 16)
                pool.wait_ge(S("listed"), 96 * (i + 1))
                pool.wait_ge(S("h_stored"), 48 * (i + 1))

            def experts(L):
                def marked(i):
                    pool.tensor_tensor(flag[L][i], C("eps"), C("eps"), ALU.add).then_inc(S(f"picked{L}"), 1)

                pool.wait_ge(S(f"npass{L}"), 1)
                npr = pool.value_load(npass[0:1, L:L + 1], min_val=0, max_val=PASSES - 1) + 1
                with pool.Fori(0, npr) as p:
                    for half in range(2):
                        src = dram_l[L].rearrange("(h a) r -> h (a r)", h=2)[
                            half:half + 1, bass.ds(p * (CAP * PAIRS * 3), CAP * PAIRS * 3)]
                        pool.dma_start(Lt_[64 * half:64 * half + 64, 0:3 * PAIRS],
                                       src.rearrange("h (s n) -> (h s) n", s=CAP)).then_inc(S(f"list_in{L}"), 16)
                    pool.wait_ge(S(f"list_in{L}"), p * 32 + 32)
                    marked(4)

                    def pick(u, col):
                        pool.tensor_copy(tok_i[u], Lt_[:, bass.ds(col, 1)]).then_inc(S(f"picked{L}"), 1)
                        pool.tensor_copy(gate_c[u].bitcast(I32), Lt_[:, bass.ds(col + 2, 1)]) \
                            .then_inc(S(f"picked{L}"), 1)

                    def gather(u):
                        pool.indirect_dma_start(out=xg[u], out_offset=None, in_=dram_h[L],
                                                in_offset=bass.IndirectOffsetOnAxis(ap=tok_i[u].bitcast(U32), axis=0),
                                                bounds_check=T - 1, oob_is_err=False) \
                            .then_inc(S(f"gathered{L}{u}"), 16)

                    per = 7 * PAIRS + 7
                    pick(0, 0)
                    pick(1, 3)
                    pool.wait_ge(S(f"picked{L}"), per * p + 5)
                    marked(4)
                    gather(0)
                    gather(1)
                    with pool.Fori(0, PAIRS // 2) as i:
                        it = p * (PAIRS // 2) + i
                        for u in range(2):
                            at = per * p + i * 14 + (7 * u + 6)
                            pool.wait_ge(S(f"x_turned{L}"), 4 * it + (2 * u + 2))
                            pool.wait_ge(S(f"act_ready{L}"), 2 * it + (u + 1))
                            marked(0)
                            pick(u, i * 6 + (3 * u + 6))
                            pool.wait_ge(S(f"picked{L}"), at + 3)
                            marked(1)
                            gather(u)
                            pool.wait_ge(S(f"scattered{L}"), 32 * it + (16 * u + 32))
                            marked(2)
                            pool.tensor_copy(pair_i[u], Lt_[:, bass.ds(i * 6 + (3 * u + 1), 1)]) \
                                .then_inc(S(f"picked{L}"), 1)
                            pool.wait_ge(S(f"picked{L}"), at + 6)
                            pool.wait_ge(S(f"y_out_a{L}"), 2 * it + u + 2)
                            pool.wait_ge(S(f"y_out_d{L}"), 2 * it + u + 2)
                            marked(3)
                            pool.indirect_dma_start(out=dram_y[L], out_offset=bass.IndirectOffsetOnAxis(
                                ap=pair_i[u].bitcast(U32), axis=0), in_=yo[u], in_offset=None,
                                bounds_check=2 * T - 1, oob_is_err=False).then_inc(S(f"scattered{L}"), 16)
                    for u in range(2):
                        pool.wait_ge(S(f"gathered{L}{u}"), p * (8 * PAIRS + 16) + (8 * PAIRS + 16))
                    pool.wait_ge(S(f"scattered{L}"), p * (16 * PAIRS) + (16 * PAIRS + 32))
                    marked(5)
                for b, (t0, n) in enumerate(BLK):
                    pool.dma_start(yl[b][0:n, :], dram_y[L][2 * t0:2 * (t0 + n), :]
                                   .rearrange("(t k) n -> t (k n)", k=2)).then_inc(S("rows_in"), 16)

            pool.wait_ge(S("const_in"), 32)
            for i in range(2):
                pool.dma_start(dram_l[i].rearrange("(p a) r -> p (a r)", p=P), a["lfill"]) \
                    .then_inc(S("lists_filled"), 16)
            pool.dma_start(stc, a["stc"]).then_inc(S("states_in"), 16)
            store_memory()
            pool.wait_ge(S("conv_out"), 8)
            pool.dma_start(a["out_cvp"], cvp).then_inc(S("conv_stored"), 16)
            pool.dma_start(a["out_cvs"], cvs).then_inc(S("conv_stored"), 16)
            pool.wait_ge(S("conv_stored"), 32)
            route(0)
            experts(0)
            memory_back()
            for h in range(H):
                for q in range(2):
                    pool.wait_ge(S("r_var"), 2 * h + q + 1)
                    pool.tensor_tensor(gv[:, 0:1], mv[:, 1:2], C("neghalf"), ALU.pow).then_inc(S("r_pow"), 1)
                pool.wait_ge(S("r_s2out"), 2 * h + 2)
                pool.dma_start(a["out_rp"][h], s1).then_inc(S("ret_stored"), 16)
            for n in range(NB * H):
                if n >= 2:
                    pool.wait_ge(S("d_add"), 2 * (n - 1))
                if n == 0:
                    pool.wait_ge(S("r_head"), 4)
                pool.tensor_scalar(kvar[n % 2], kdec, C("kvmask")[:, n:n + 1], None, ALU.mult) \
                    .then_inc(S("kvar_ready"), 1)
                if n % H == 3 and n > 3:
                    store_state(n // H - 1)
            store_state(NB - 1)
            pool.wait_ge(S("r_var"), 9)
            pool.tensor_tensor(gv[:, 0:1], mv[:, 1:2], C("neghalf"), ALU.pow).then_inc(S("r_pow"), 1)
            route(1)
            experts(1)
            pool.wait_ge(S("normed"), NORM_DONE["final"])
            pool.dma_start(a["out_y"], hT).then_inc(S("y_stored"), 16)
            pool.wait_ge(S("y_stored"), 16)
            pool.wait_ge(S("conv_stored"), 32)
            pool.wait_ge(S("ret_stored"), 16 * H)
            for i in range(2):
                pool.wait_ge(S(f"keys_stored{i}"), 16)
                pool.wait_ge(S(f"values_stored{i}"), 16)
            for b in range(2):
                pool.wait_ge(S(f"state_stored{b}"), 16 * NB // 2)


OUTS = {"out_y": (P, KD, T), "out_cvp": (P, 8, 2), "out_cvs": (P, 8, 16), "out_rp": (H, P, 2, DV),
        "out_rs": (NB, P, 8, DV), "out_mk": (2, NM, D), "out_mv": (2, NM, D)}


def feature_major(v, k):
    return np.ascontiguousarray(v.reshape(-1, k, P).transpose(2, 1, 0))


def tiles(w, kt, per):
    n = w.shape[1] // P
    w = w.reshape(kt, P, n // per, per, P)
    return np.ascontiguousarray(w.transpose(2, 1, 3, 0, 4).reshape(n // per, P, per * kt * P))


def constants():
    f = np.float32
    c = np.zeros((P, NCC), f)

    def put(name, v):
        o, w = CC[name]
        c[:, o:o + w] = v

    i = np.arange(P)
    put("ident", np.eye(P))
    put("ones", 1.0)
    put("tri", (i[:, None] < i[None, :]))
    e = np.arange(NE)
    put("iota", e)
    put("cexp", (e % 2) * LROW + e // 2)
    pos = np.concatenate([np.arange(TP), np.tile(PAST + np.arange(NS), NB)]).astype(f)
    inv = np.power(f(10000.0), -np.arange(P, dtype=f) / f(P)).astype(f)
    ang = (pos[None, :] * inv[:, None]).astype(f).astype(np.float64)
    put("cos", np.cos(ang))
    put("sin", np.sin(ang))
    lg = np.array(LOGG)
    diff = i[None, :] - i[:, None]
    decay = np.where(diff >= 0, np.exp(np.maximum(diff, 0)[None] * lg[:, None, None]), 0.0) / 16.0
    put("decay", decay.transpose(1, 0, 2).reshape(P, -1))
    t = np.arange(TD)
    same = (t[:, None] // NS == t[None, :] // NS) & (t[None, :] >= t[:, None])
    dm = np.where(same, np.exp((t[None, :] - t[:, None])[None] * lg[:, None, None] * same), 0.0) / 16.0
    put("dmask", dm.reshape(P, TD))
    put("inner", np.exp((i + 1)[None, :] * lg[:, None]).reshape(1, -1))
    put("tail", np.exp((P - 1 - i)[:, None] * lg[None, :]) / 16.0)
    put("tdec", (np.exp((NS - 1 - t % NS)[None, :] * lg[:, None]) / 16.0).reshape(P, 1))
    h, b = i // TD, (i % TD) // NS
    n = np.arange(NB * H)
    put("kvmask", (b[:, None] == n[None, :] // H) & (h[:, None] == n[None, :] % H))
    put("neghalf", -0.5)
    put("eps", EPS)
    tok = np.arange(3)[None, :] * P + i[:, None]
    put("valid", tok < T)
    put("far", np.where(tok < T, 0, FAR))
    put("thr", CAP * np.arange(1, PASSES))
    o = CC["tok"][0]
    c.view(np.int32)[:, o:o + 6] = np.repeat(tok, 2, 1)
    o = CC["pair"][0]
    c.view(np.int32)[:, o:o + 6] = np.repeat(2 * tok, 2, 1) + np.tile([0, 1], 3)[None, :]
    return c


def lay_out(x):
    o = {"cst": constants()}
    o["xT"] = feature_major(np.concatenate([x["x_prompt"][0], x["x_sample"].reshape(TD, D)]), KD)
    o["memT"] = feature_major(x["mem_prompt"][0], KD)
    cols = [x["norm_mix"][0], x["norm_mix"][1], x["norm_ffn"][0], x["norm_ffn"][1], x["mem_norm"][0],
            x["mem_norm"][1], x["final_norm"], x["ret_gn"][0]]
    par = [c.reshape(-1, P).T for c in cols] + [x["conv_w"][0].reshape(3, 8, P).transpose(2, 1, 0).reshape(P, 24)]
    o["par"] = np.ascontiguousarray(np.concatenate(par, 1))
    o["wkv"] = np.ascontiguousarray(x["w_mem_kv"].reshape(2, KD, P, 4, 512).transpose(0, 3, 2, 1, 4)
                                    .reshape(8, P, SLOT))
    w = x["conv_w_in"][0].reshape(D, 4, 8, P)
    o["cin"] = tiles(w.transpose(0, 2, 1, 3)[:, :, [1, 2, 0, 3]].reshape(D, -1), KD, 4)
    o["cout"] = tiles(x["conv_w_out"][0], 16, 2)
    w = x["ret_w_in"][0]
    heads = []
    for h in range(H):
        heads += [w[:, 256 * h:256 * h + 256], w[:, 1024 + 256 * h:1280 + 256 * h],
                  w[:, 2048 + DV * h:2048 + DV * h + DV], w[:, 4096 + DV * h:4096 + DV * h + DV]]
    o["rin"] = tiles(np.concatenate(heads + [w[:, 6144:]], 1), KD, 4)
    o["rout"] = tiles(x["ret_w_out"][0], 24, 1)
    o["kc"] = np.ascontiguousarray(x["cache_mem_k"].reshape(2, 4, 2, NM, 8, P).transpose(0, 1, 5, 2, 4, 3)
                                   .reshape(8, P, SLOT))
    o["vc"] = np.ascontiguousarray(x["cache_mem_v"].reshape(2, 4, 2, 2, P, D).transpose(0, 1, 4, 2, 3, 5)
                                   .reshape(8, P, SLOT))
    o["st"] = np.ascontiguousarray(x["state_ret"][0].reshape(NB, H, 2, P, DV).transpose(0, 3, 1, 2, 4)
                                   .reshape(NB, P, SLOT))
    o["stc"] = np.ascontiguousarray(x["state_conv"][0].reshape(NB, 2, 8, P).transpose(3, 2, 0, 1).reshape(P, 8, 16))
    w = np.concatenate([x["moe_w_group"], x["moe_w_router"]], 2)
    o["wr"] = np.ascontiguousarray(w.reshape(2, KD, P, NG + NE).transpose(0, 2, 1, 3).reshape(2, P, KD * 36))
    o["gu"] = np.ascontiguousarray(x["moe_w_gate_up"].reshape(2 * NE, KD, P, 2 * FF).transpose(0, 2, 1, 3)
                                   .reshape(2 * NE, P, SLOT))
    o["dn"] = np.ascontiguousarray(x["moe_w_down"].reshape(2 * PAIRS, 2, 2, P, D).transpose(0, 3, 1, 2, 4)
                                   .reshape(2 * PAIRS, P, SLOT))
    fill = np.zeros((2 * LROW, 3), np.int32)
    fill[:, 0:2] = FAR
    o["lfill"] = np.ascontiguousarray(fill.reshape(P, -1))
    return o


def unpack(r):
    y = r["out_y"].transpose(2, 1, 0).reshape(T, D)
    cvp = r["out_cvp"].transpose(2, 1, 0).reshape(1, 1, 2, D)
    cvs = r["out_cvs"].reshape(P, 8, NB, 2).transpose(2, 3, 1, 0).reshape(1, NB, 2, D)
    rp = r["out_rp"].transpose(0, 2, 1, 3).reshape(1, 1, H, 256, DV)
    rs = r["out_rs"].reshape(NB, P, H, 2, DV).transpose(0, 2, 3, 1, 4).reshape(1, NB, H, 256, DV)
    mk = r["out_mk"].reshape(2, 1, NM, H, 256)
    mv = r["out_mv"].reshape(2, 1, NM, H, 256)
    return tuple(np.ascontiguousarray(v) for v in
                 (y[:TP].reshape(1, TP, D), y[TP:].reshape(NB, NS, D), cvp, cvs, rp, rs, mk, mv))


def kernel(**inputs):
    import concourse.bacc as bacc
    from concourse.bass_utils import run_bass_kernel_spmd

    x = {k: np.asarray(v) for k, v in inputs.items()}
    arrays = lay_out(x)
    nc = bacc.Bacc("TRN2", target_bir_lowering=False, num_devices=1)
    a = {n: nc.dram_tensor("in_" + n, v.shape, mybir.dt.from_np(v.dtype), kind="ExternalInput").ap()
         for n, v in arrays.items()}
    for n, shape in OUTS.items():
        a[n] = nc.dram_tensor(n, shape, F32, kind="ExternalOutput").ap()
    build(nc, a)
    r = run_bass_kernel_spmd(nc, [{"in_" + n: v for n, v in arrays.items()}], core_ids=[0])
    return unpack({n: r.results[0][n] for n in OUTS})
```

```python
from contextlib import ExitStack

import numpy as np

import concourse.bass as bass
from concourse import mybir

F32 = mybir.dt.float32
I32 = mybir.dt.int32
U32 = mybir.dt.uint32
ALU = mybir.AluOpType
ACT = mybir.ActivationFunctionType
AX = mybir.AxisListType

P = 128
D = 1024
KD = D // P
TP, NB, NS = 256, 8, 4
TD = NB * NS
T = TP + TD
PAST = 2048
NM = 256
H = 4
DV = 512
FF = 256
NE, NG = 32, 4
EPG = NE // NG
EPS = 1e-6
SLOT = 4096
R = 6
CAP = 64
PASSES = -(-T // CAP)
PAIRS = NE // 2
LROW = PASSES * CAP * PAIRS
FAR = 1 << 20
BIG = 3.0e38
BLK = [(0, 128), (128, 128), (256, 32)]
LOGG = [float(np.log1p(-np.exp2(-5.0 - h))) for h in range(H)]

SEQ_A = ([("kv0", c) for c in range(4)] + [("cin", c) for c in range(8)] + [("kc0", c) for c in range(4)]
         + [("vc0", c) for c in range(4)] + [("cout", c) for c in range(4)] + [("kv1", c) for c in (0, 1)])
QUERY_AFTER = {1: 12, 3: 13}
SEQ_B = ([("kv1", c) for c in (2, 3)] + [("rin", c) for c in range(12)]
         + [x for b in range(NB) for x in [("st", b)] + ([("rin", QUERY_AFTER[b])] if b in QUERY_AFTER else [])]
         + [("kc1", c) for c in range(4)] + [("vc1", c) for c in range(4)] + [("rout", c) for c in range(8)])
OFF_A = 0
OFF_M0 = len(SEQ_A) % R
OFF_B = OFF_M0
OFF_M1 = (OFF_B + len(SEQ_B)) % R


def constant_columns():
    cols = [("ident", P), ("ones", P), ("tri", P), ("iota", NE), ("cexp", NE), ("cos", T), ("sin", T),
            ("decay", H * P), ("dmask", TD), ("inner", H * P), ("tail", H), ("tdec", 1), ("kvmask", NB * H),
            ("neghalf", 1), ("eps", 1), ("valid", 3), ("far", 3), ("thr", 4), ("pair", 6), ("slots", CAP)]
    at, out = 0, {}
    for n, w in cols:
        out[n] = (at, w)
        at += w
    return out, at


def parameter_columns():
    cols = [("mix0", 8), ("mix1", 8), ("ffn0", 8), ("ffn1", 8), ("mem0", 8), ("mem1", 8), ("final", 8),
            ("gn", 16), ("cw", 24)]
    at, out = 0, {}
    for n, w in cols:
        out[n] = (at, w)
        at += w
    return out, at


CC, NCC = constant_columns()
PC, NPC = parameter_columns()


def build(nc, a):
    dram_y = [nc.dram_tensor(f"expert_rows{i}", (2 * T, D), F32).ap() for i in range(2)]
    dram_l = [nc.dram_tensor(f"expert_lists{i}", (2 * LROW, 2), I32).ap() for i in range(2)]

    with ExitStack() as ctx:
        def sb(name, words, dt=F32):
            return ctx.enter_context(nc.sbuf_tensor(name, [P, words], dt))

        sems = {}

        def S(name):
            if name not in sems:
                sems[name] = ctx.enter_context(nc.semaphore(name))
            return sems[name]

        ring = sb("ring", R * SLOT)
        cst = sb("cst", NCC)
        par = sb("par", NPC)
        xT_ = sb("xT", KD * T)
        hT_ = sb("hT", KD * T)
        small = sb("small", 96)
        arena = sb("arena", 21568)
        bank = [ctx.enter_context(nc.psum_tensor(f"bank{i}", [P, 512], F32)) for i in range(8)]

        def C(name, rows=P):
            o, w = CC[name]
            return cst[0:rows, o:o + w]

        def G(name):
            o, w = PC[name]
            return par[:, o:o + w]

        def ar(off, n):
            return arena[:, off:off + n]

        def v3(ap, k):
            return ap.rearrange("p (k t) -> p k t", k=k)

        HM1, KTO, VO, SQO, CATO, PHO, QMO, MSO = 0, 2048, 4096, 6144, 8448, 15360, 18688, 20992
        xT, hT = v3(xT_[:, :], KD), v3(hT_[:, :], KD)
        hm1 = v3(ar(HM1, KD * NM), KD)
        KT = v3(ar(KTO, 2048), 8)
        V = v3(ar(VO, 2048), 2)
        sq = v3(ar(SQO, KD * T), KD)
        cat = v3(ar(CATO, 24 * T), 24)
        memT = v3(ar(CATO, KD * NM), KD)
        hm0 = v3(ar(CATO + 2048, KD * NM), KD)
        Ktok = v3(ar(PHO, 2048), 2)
        keys1 = v3(hT_[:, 0:2048], 2)
        qx = v3(ar(PHO, 8 * T), 8)
        qm_ = ar(QMO, 8 * T)
        qm = v3(qm_, 8)
        qm_diag = qm.rearrange("p h (b x) -> p h b x", x=TD + NS)[:, :, :, 0:NS]
        c_sb = [ar(SQO + 288 * i, T) for i in range(2)]
        full = [ar(SQO + 576 + 306 * i, 306) for i in range(2)]
        yc = [ar(SQO + 1188 + 288 * i, T) for i in range(2)]
        stc = v3(ar(PHO + 2304, 128), 8)
        cvp = v3(ar(PHO + 2432, 16), 8)
        cvs = v3(ar(PHO + 2448, 128), 8)
        Pm = [hT_[:, 256 * i:256 * i + 256] for i in range(2)]
        PT = [v3(hT_[:, 512 + 512 * i:1024 + 512 * i], 2) for i in range(2)]
        od = hT_[:, 1536:1792]
        mx, nb_, rs, rr = (small[:, 9 * i:9 * i + 9] for i in range(4))
        qTh, kTh = v3(ar(PHO, 576), 2), v3(ar(PHO + 576, 576), 2)
        vTh = v3(ar(PHO + 1152, 1152), 4)
        vtok = v3(ar(PHO + 2304, 1024), 2)
        kvar = [ar(PHO + 2304 + 256 * i, 256) for i in range(2)]
        s1, on = v3(ar(HM1, 1024), 2), v3(ar(HM1 + 1024, 1024), 2)
        ktail, ST, qin = v3(ar(SQO, 512), 2), v3(ar(SQO + 512, 256), 2), v3(ar(SQO + 768, 256), 2)
        vdec, kdec, STd = ar(SQO + 1024, 512), ar(SQO + 1536, 256), ar(SQO + 1792, 128)
        rot = ar(SQO + 1920, 288)
        th = [ar(MSO + 288 * i, T) for i in range(2)]
        bn6, mv, gv = small[:, 36:48], small[:, 48:52], small[:, 52:54]
        nrm = ar(MSO, 576)
        ms, rstd = nrm[:, 0:288], nrm[:, 288:576]
        ro = [PHO]

        def rt(n, dt=F32):
            x = ar(ro[0], n)
            ro[0] += n
            return x if dt == F32 else x.bitcast(dt)

        rl = v3(rt(108), 3)
        lgp, gm8, em8, e8 = (v3(rt(24), 3) for _ in range(4))
        gi8, ei8 = (v3(rt(24, U32), 3) for _ in range(2))
        g4 = v3(rt(12), 3)
        gf, ng, ne, gs, es, fr = (rt(3) for _ in range(6))
        pen = v3(rt(12), 3)
        lem = rt(96).rearrange("p (b g e) -> p b g e", b=3, g=NG)
        ef, pe2, idxf = (v3(rt(6), 3) for _ in range(3))
        oh = rt(192).rearrange("p (b k e) -> p b k e", b=3, k=2)
        prod = rt(192).rearrange("p (b k e) -> p b k e", b=3, k=2)
        M, Gx = v3(rt(96), 3), v3(rt(96), 3)
        idxi = v3(rt(6, I32), 3)
        rec = rt(12, I32).rearrange("p (b k r) -> p b k r", b=3, k=2)
        rec_gate = rec.bitcast(F32)[:, :, :, 1]
        cmx, cgt, npf = rt(1), rt(4), rt(1)
        rk_ = rt(3 * (NE + 4))
        rk = v3(rk_, 3)
        Lt_ = rt(2 * PAIRS + 4, I32)
        wr_sb = rt(288)
        pair_i = [small[:, 66 + u:67 + u].bitcast(I32) for u in range(2)]
        gate_c = [small[:, 68 + u:69 + u] for u in range(2)]
        npass = small[:, 60:62].bitcast(I32)
        flag = [[small[:, 74 + 6 * l + i:75 + 6 * l + i] for i in range(6)] for l in range(2)]
        assert ro[0] <= QMO
        htok = [ar(CATO + 1024 * i, 1024) for i in range(3)]
        onehot = [ar(KTO + 3 * P * i, 3 * P).rearrange("p (b s) -> p b s", b=3) for i in range(2)]
        xgT = [v3(ar(VO + 1024 * i, 1024), 8) for i in range(2)]
        yo = [ar(CATO + 3072 + 1024 * i, 1024) for i in range(2)]
        act_ = [ar(CATO + 5120 + 256 * i, 256) for i in range(2)]
        actT = [v3(ar(CATO + 5632 + 256 * i, 256), 2) for i in range(2)]
        tg = [ar(CATO + 6144 + 256 * i, 256) for i in range(2)]
        yl = [ar(CATO + 2048 * i, 2048) for i in range(3)]

        def slot(s):
            return ring[:, s * SLOT:(s + 1) * SLOT]

        def part(name):
            seq, off, tag = (SEQ_A, OFF_A, "A") if name in SEQ_A else (SEQ_B, OFF_B, "B")
            n = seq.index(name)
            return tag, n, (n + off) % R

        def uses_before(tag, s):
            return 0 if tag == "A" else sum((n + OFF_A) % R == s for n in range(len(SEQ_A)))

        def landed(eng, name):
            tag, n, s = part(name)
            eng.wait_ge(S(f"landed{s}"), 16 * (n // R + 1 + uses_before(tag, s)))
            return slot(s)

        def chain(eng, key, ins):
            counts[key] = counts.get(key, 0) + 1
            ins.then_inc(S(key), 1)
            eng.wait_ge(S(key), counts[key])

        def rin_banks(c):
            return [bank[(4, 0, 4)[c % 3] + o][:, 0:T] for o in range(4)] if c < 12 else \
                [bank[i][:, 0:T] for i in (5, 6, 7, 4)]

        counts = {}
        block = ctx.enter_context(nc.Block())

        NORM = {"mem": 0, "mix0": 1, "ffn0": 2, "mix1": 3, "ffn1": 4, "final": 5}
        NORM_DONE = {"mem": 16, "mix0": 24, "ffn0": 32, "mix1": 40, "ffn1": 48, "final": 56}

        def wait_used(eng, name):
            k, c = name
            sem, v = {"kv0": ("kv_sum", 2 * (c + 1)), "kv1": ("kv_sum", 8 + 2 * (c + 1)),
                      "cin": ("cin_sum", 4 * (c + 1)), "rin": ("rin_sum", 4 * (c + 1)),
                      "kc0": ("dec_scores", c + 1), "kc1": ("dec_scores", 4 + c + 1),
                      "vc0": ("dec_pv", c + 1), "vc1": ("dec_pv", 4 + c + 1),
                      "cout": ("proj", 2 * (c + 1)), "rout": ("proj", 8 + c + 1),
                      "st": (f"state_stored{c % 2}", 16 * (c // 2 + 1))}[k]
            eng.wait_ge(S(sem), v)

        @block.sync
        def _(sp):
            sp.dma_start(memT, a["memT"]).then_inc(S("mem_in"), 16)
            sp.dma_start(cst[:, :], a["cst"]).then_inc(S("const_in"), 16)
            sp.dma_start(par[:, :], a["par"]).then_inc(S("const_in"), 16)

            def source(name):
                k, c = name
                if k in ("kv0", "kv1"):
                    return a["wkv"][4 * int(k[2]) + c]
                if k in ("kc0", "kc1", "vc0", "vc1"):
                    return a[k[0] + "c"][4 * int(k[2]) + c]
                return a[k][c]

            def stream(seq, tag, off, before):
                for n, name in enumerate(seq):
                    s = (n + off) % R
                    if n < R:
                        before(n)
                    else:
                        wait_used(sp, seq[n - R])
                    src = source(name)
                    sp.dma_start(slot(s)[:, 0:src.shape[1]], src).then_inc(S(f"landed{s}"), 16)
                    if tag == "A" and n == 0:
                        sp.dma_start(xT, a["xT"]).then_inc(S("x_in"), 16)

            def experts(L, off, seq):
                def body(first, i, it):
                    for j in range(R):
                        u, c = divmod(j, 3)
                        s = (off + j) % R
                        if first:
                            wait_used(sp, seq[len(seq) - R + j])
                        elif c < 2:
                            sp.wait_ge(S(f"gu_sum{L}"), 2 * it - 1 + u)
                        else:
                            sp.wait_ge(S(f"y_sum{L}"), 4 * it - 2 + 2 * u)
                        if c < 2:
                            src = a["gu"][bass.ds(4 * i + (L * NE + 2 * u + c), 1)]
                        else:
                            src = a["dn"][bass.ds(2 * i + (L * PAIRS + u), 1)]
                        sp.dma_start(slot(s), src.rearrange("a p n -> p (a n)")) \
                          .then_inc(S(f"landed_M{L}{s}"), 16)
                body(True, 0, 0)
                with sp.Fori(1, PAIRS // 2) as i:
                    body(False, i, i)
                sp.wait_ge(S(f"npass{L}"), 1)
                more = sp.value_load(npass[0:1, L:L + 1], min_val=0, max_val=PASSES - 1)
                with sp.If(more > 0):
                    with sp.Fori(0, more) as p:
                        with sp.Fori(0, PAIRS // 2) as i:
                            body(False, i, p * (PAIRS // 2) + PAIRS // 2 + i)
                return more

            stream(SEQ_A, "A", OFF_A, lambda n: None)
            more0 = experts(0, OFF_M0, SEQ_A)

            def after_experts(n):
                u, c = divmod(n, 3)
                if n == 2:
                    for b in range(3):
                        sp.wait_ge(S(f"rows_in{b}"), 16)
                if c < 2:
                    sp.wait_ge(S("gu_sum0"), more0 * PAIRS + (PAIRS - 1 + u))
                else:
                    sp.wait_ge(S("y_sum0"), more0 * (2 * PAIRS) + (2 * PAIRS - 2 + 2 * u))

            stream(SEQ_B, "B", OFF_B, after_experts)
            experts(1, OFF_M1, SEQ_B)

        @block.tensor
        def _(pe):
            def norm_sum(name, n, ks=range(KD)):
                for k in ks:
                    pe.wait_ge(S("squared"), KD * NORM[name] + k + 1)
                    mm = pe.matmul(bank[7][:, 0:n], C("ones"), sq[:, k, 0:n], start=(k == 0), stop=(k == KD - 1))
                if ks[-1] == KD - 1:
                    mm.then_inc(S("sumsq"), 1)

            KV_BANKS = ((0, 1, 2, 3, 4, 5, 6, 7), (4, 7, 0, 1, 4, 7, 5, 6))
            KT_BANKS = ((0, 1, 2, 3), (4, 5, 6, 0))

            def memory_kv(i, j):
                c, mb = divmod(j, 2)
                src = (hm0, hm1)[i]
                w = v3(landed(pe, (f"kv{i}", c)), KD)
                for k in range(KD):
                    if i == 0 and j == 0:
                        pe.wait_ge(S("normed"), k + 1)
                    mm = pe.matmul(bank[KV_BANKS[i][j]][:, :], src[:, k, mb * P:(mb + 1) * P], w[:, k, :],
                                   start=(k == 0), stop=(k == KD - 1))
                mm.then_inc(S("kv_sum"), 1)

            def turn_keys(i):
                for g in range(4):
                    for hd in range(2):
                        for mb in range(2):
                            mm = pe.transpose(bank[KT_BANKS[i][g]][:, hd * 256 + mb * P:hd * 256 + (mb + 1) * P],
                                              Ktok[:, mb, (2 * g + hd) * P:(2 * g + hd + 1) * P], C("ident"))
                    mm.then_inc(S("kt_turned"), 1)

            def attention(i):
                pe.wait_ge(S("qmask_x"), i + 1)
                for c in range(4):
                    k2 = landed(pe, (f"kc{i}", c)).rearrange("p (b h m) -> p b h m", b=2, h=8)
                    for bi in range(2):
                        for dt in range(2):
                            for h in range(H):
                                b = 2 * c + bi
                                mm = pe.matmul(bank[0][32 * h:32 * h + 32, 0:NM],
                                               qm[:, 2 * h + dt, 32 * b:32 * b + 32], k2[:, bi, 2 * h + dt, :],
                                               start=(b == 0 and dt == 0), stop=(b == NB - 1 and dt == 1),
                                               skip_group_check=True)
                    mm.then_inc(S("dec_scores"), 1)
                jobs = [None] + [(h, tb) for h in range(H) for tb in range(2)]

                def scores(j):
                    h, tb = jobs[j]
                    if j > 2:
                        pe.wait_ge(S("exp_done"), 9 * i + j - 1)
                    for dt in range(2):
                        mm = pe.matmul(bank[1 + (j - 1) % 2][:, 0:NM], qx[:, 2 * h + dt, tb * P:(tb + 1) * P],
                                       KT[:, 2 * h + dt, :], start=(dt == 0), stop=(dt == 1))
                    mm.then_inc(S("pr_scores"), 1)

                def turn(j):
                    pe.wait_ge(S("p_ready"), 9 * i + j + 1)
                    if j == 2:
                        pe.wait_ge(S("pt0_out"), i + 1)
                    if j > 2:
                        pe.wait_ge(S("pt_out"), 8 * i + j - 2)
                    for mb in range(2):
                        mm = pe.transpose(bank[3 + j % 2][:, mb * P:(mb + 1) * P], Pm[j % 2][:, mb * P:(mb + 1) * P],
                                          C("ident"))
                    mm.then_inc(S("p_turned"), 1)

                def pv(h):
                    pe.wait_ge(S("pt_out"), 8 * i + 2 * h + 2)
                    if h >= 2:
                        pe.wait_ge(S("pv_out"), 4 * i + h - 1)
                    for dt in range(2):
                        for mb in range(2):
                            mm = pe.matmul(bank[5 + h % 2][:, dt * TP:(dt + 1) * TP],
                                           V[:, mb, (2 * h + dt) * P:(2 * h + dt + 1) * P], PT[h % 2][:, mb, :],
                                           start=(mb == 0), stop=(mb == 1))
                    mm.then_inc(S("pv_sum"), 1)

                scores(1)
                scores(2)
                for j in range(9):
                    turn(j)
                    if j + 3 <= 8:
                        scores(j + 3)
                    if j >= 3 and j % 2 == 1:
                        pv((j - 3) // 2)
                pv(3)
                for c in range(4):
                    v2 = landed(pe, (f"vc{i}", c)).rearrange("p (b q n) -> p b q n", b=2, q=2)
                    if c == 0:
                        pe.wait_ge(S("pt0_out"), i + 1)
                    for bi in range(2):
                        for mb in range(2):
                            for h in range(H):
                                b = 2 * c + bi
                                mm = pe.matmul(bank[7][32 * h:32 * h + 32, 0:NM],
                                               qm[:, 4 * mb + h, 32 * b:32 * b + 32],
                                               v2[:, bi, mb, h * 256:(h + 1) * 256],
                                               start=(b == 0 and mb == 0), stop=(b == NB - 1 and mb == 1),
                                               skip_group_check=True)
                    mm.then_inc(S("dec_pv"), 1)
                pe.wait_ge(S("od_out"), i + 1)
                for dt in range(2):
                    mm = pe.transpose(bank[0][:, dt * P:(dt + 1) * P], od[:, dt * P:(dt + 1) * P], C("ident"))
                mm.then_inc(S("od_turned"), 1)

            def project_out(i, kt):
                name, per = (("cout", 2), ("rout", 1))[i]
                for o in range(KD):
                    w = v3(landed(pe, (name, o // per))[:, (o % per) * kt * P:(o % per + 1) * kt * P], kt)
                    if o == 0:
                        pe.wait_ge(S("cat_ready"), i + 1)
                    if o >= 4:
                        pe.wait_ge(S("res_add"), 8 * i + o - 3)
                    for k in range(kt):
                        mm = pe.matmul(bank[1 + o % 4][:, 0:T], w[:, k, :], cat[:, k, :],
                                       start=(k == 0), stop=(k == kt - 1))
                    mm.then_inc(S("proj"), 1)
                    if o >= 2:
                        norm_sum(f"ffn{i}", T, [o - 2])
                norm_sum(f"ffn{i}", T, [KD - 2, KD - 1])

            def route(i):
                pe.wait_ge(S("router_in"), 16 * (i + 1))
                wr = v3(wr_sb, KD)
                for b, (t0, n) in enumerate(BLK):
                    for k in range(KD):
                        if b == 0:
                            pe.wait_ge(S("normed"), NORM_DONE[f"ffn{i}"] - KD + k + 1)
                        mm = pe.matmul(bank[6][0:n, b * 36:b * 36 + 36], hT[:, k, t0:t0 + n], wr[:, k, :],
                                       start=(k == 0), stop=(k == KD - 1))
                mm.then_inc(S("logits"), 1)
                for j in range(6):
                    b, half = divmod(j, 2)
                    t0, n = BLK[b]
                    if j >= 4:
                        pe.wait_ge(S("htok_out"), 6 * i + j - 3)
                    for k in range(4):
                        mm = pe.transpose(bank[j % 4][0:n, k * P:(k + 1) * P], hT[:, 4 * half + k, t0:t0 + n],
                                          C("ident"))
                    mm.then_inc(S("h_turned"), 1)
                if i == 0:
                    memory_kv(1, 0)
                pe.wait_ge(S("chosen"), i + 1)
                for b in range(3):
                    for bb in range(b + 1):
                        mm = pe.matmul(bank[5][:, b * NE:(b + 1) * NE], C("tri") if bb == b else C("ones"),
                                       M[:, bb, :], start=(bb == 0), stop=(bb == b))
                for bb in range(3):
                    mm = pe.matmul(bank[5][:, 3 * NE:4 * NE], C("ones"), M[:, bb, :], start=(bb == 0), stop=(bb == 2))
                mm.then_inc(S("ranks"), 1)
                if i == 0:
                    memory_kv(1, 1)
                pe.wait_ge(S("htok_out"), 6 * (i + 1))
                if i == 0:
                    memory_kv(1, 2)
                    memory_kv(1, 3)
                    pe.wait_ge(S("kv1_out"), 4)

            def experts(L, off):
                pe.wait_ge(S(f"npass{L}"), 1)
                npr = pe.value_load(npass[0:1, L:L + 1], min_val=0, max_val=PASSES - 1) + 1

                def pick(p, it, u):
                    pe.wait_ge(S(f"selected{L}"), 2 * it + u + 2 * p + 1)
                    for k in range(KD):
                        for b, (t0, n) in enumerate(BLK):
                            mm = pe.matmul(bank[k // 4][:, (k % 4) * P:(k % 4 + 1) * P],
                                           htok[b][0:n, k * P:(k + 1) * P], onehot[u][0:n, b, :],
                                           start=(b == 0), stop=(b == 2), skip_group_check=True)
                        if k % 4 == 3:
                            mm.then_inc(S(f"x_picked{L}"), 1)

                def pair(p, i, u, more):
                    it = p * (PAIRS // 2) + i
                    g = 2 * it + u
                    w = []
                    for c in range(2):
                        s = (off + 3 * u + c) % R
                        pe.wait_ge(S(f"landed_M{L}{s}"), 16 * it + 16)
                        w.append(v3(slot(s), KD))
                    pe.wait_ge(S(f"xt_out_a{L}"), g + 1)
                    pe.wait_ge(S(f"xt_out_d{L}"), g + 1)
                    for k in range(KD):
                        for c in range(2):
                            mm = pe.matmul(bank[2 + u][64 * c:64 * c + 64, :], xgT[u][:, k, 64 * c:64 * c + 64],
                                           w[c][:, k, :], start=(k == 0), stop=(k == KD - 1),
                                           skip_group_check=True)
                    mm.then_inc(S(f"gu_sum{L}"), 1)
                    if more:
                        pick(p, it + u, 1 - u)
                    pe.wait_ge(S(f"act_ready{L}"), g + 1)
                    for f in range(2):
                        mm = pe.transpose(bank[4][:, f * P:(f + 1) * P], act_[u][:, f * P:(f + 1) * P], C("ident"))
                    mm.then_inc(S(f"act_turned{L}"), 1)
                    s = (off + 3 * u + 2) % R
                    pe.wait_ge(S(f"landed_M{L}{s}"), 16 * it + 16)
                    wd = slot(s).rearrange("p (c f n) -> p c f n", c=2, f=2)
                    pe.wait_ge(S(f"actT_out{L}"), g + 1)
                    pe.wait_ge(S(f"y_out_a{L}"), g + 1)
                    pe.wait_ge(S(f"y_out_d{L}"), g + 1)
                    for n in range(2):
                        for f in range(2):
                            for c in range(2):
                                mm = pe.matmul(bank[5 + n][64 * c:64 * c + 64, :],
                                               actT[u][:, f, 64 * c:64 * c + 64],
                                               wd[:, c, f, n * 512:(n + 1) * 512],
                                               start=(f == 0), stop=(f == 1), skip_group_check=True)
                        mm.then_inc(S(f"y_sum{L}"), 1)

                with pe.Fori(0, npr) as p:
                    pick(p, p * (PAIRS // 2), 0)
                    with pe.Fori(0, PAIRS // 2 - 1) as i:
                        pair(p, i, 0, True)
                        pair(p, i, 1, True)
                    pair(p, PAIRS // 2 - 1, 0, True)
                    pair(p, PAIRS // 2 - 1, 1, False)
                pe.wait_ge(S(f"y_out_a{L}"), npr * PAIRS + 1)
                pe.wait_ge(S(f"y_out_d{L}"), npr * PAIRS + 1)

            def combine(L):
                for j in range(6):
                    b, half = divmod(j, 2)
                    n = BLK[b][1]
                    pe.wait_ge(S("rows_added"), 3 * L + b + 1)
                    if j >= 4:
                        pe.wait_ge(S("moe_add"), 6 * L + j - 3)
                    for k in range(4):
                        mm = pe.transpose(bank[j % 4][:, k * P:k * P + n],
                                          yl[b][0:n, (4 * half + k) * P:(4 * half + k + 1) * P], C("ident", n)[:, 0:n])
                    mm.then_inc(S("rows_turned"), 1)

            def project_in(name, c, src, drained, halfway=None, normed=None):
                outs = rin_banks(c) if name == "rin" else [bank[4 * (c % 2) + o][:, 0:T] for o in range(4)]
                w = landed(pe, (name, c)).rearrange("p (o k n) -> p o k n", o=4, k=KD)
                drained(c)
                for o in range(4):
                    if o == 2 and halfway:
                        halfway()
                    for k in range(KD):
                        if normed and o == 0:
                            pe.wait_ge(S("normed"), normed - KD + k + 1)
                        mm = pe.matmul(outs[o], w[:, o, k, :], src[:, k, :],
                                       start=(k == 0), stop=(k == KD - 1))
                    mm.then_inc(S(name + "_sum"), 1)

            pe.wait_ge(S("const_in"), 32)
            norm_sum("mem", NM)
            pe.wait_ge(S("ms_out"), 1)
            for j in range(4):
                memory_kv(0, j)
            norm_sum("mix0", T)
            for j in range(4, 8):
                if j == 7:
                    pe.wait_ge(S("ms_out"), 2)
                memory_kv(0, j)
            pe.wait_ge(S("ktok_out"), 4)
            turn_keys(0)
            pe.wait_ge(S("kt_out_a"), 2)
            pe.wait_ge(S("kt_out_d"), 2)
            pe.wait_ge(S("v_out"), 4)
            pe.wait_ge(S("normed"), NORM_DONE["mix0"])

            def conv_drained(c):
                if c >= 2:
                    pe.wait_ge(S("conv_out"), c - 1)
                    pe.wait_ge(S("qx_out0"), c - 1)

            for c in range(8):
                project_in("cin", c, hT, conv_drained)
            pe.wait_ge(S("conv_out"), 8)
            pe.wait_ge(S("qx_out0"), 8)
            attention(0)
            project_out(0, 16)
            pe.wait_ge(S("ms_out"), 3)
            route(0)
            experts(0, OFF_M0)
            for j in range(4, 8):
                memory_kv(1, j)
            combine(0)
            pe.wait_ge(S("values1_out"), 4)
            norm_sum("mix1", T)
            pe.wait_ge(S("keys_back"), 16)
            turn_keys(1)
            pe.wait_ge(S("kt_out_a"), 6)
            pe.wait_ge(S("ms_out"), 4)

            def ret_drained(c):
                if c >= 2:
                    pe.wait_ge(S("rin_out"), c - 1)
                    pe.wait_ge(S("rin_out_a"), c - 1)

            def retention(h):
                c0 = 3 * h + 2
                pe.wait_ge(S("rin_out"), c0 + 1)
                pe.wait_ge(S("rin_out_a"), c0 + 1)
                dec = slice(TP, T)
                for c in range(2):
                    for dt in range(2):
                        mm = pe.transpose(bank[0][:, (2 * c + dt) * P:(2 * c + dt + 1) * P],
                                          kTh[:, dt, c * P:(c + 1) * P], C("ident"))
                mm.then_inc(S("r_kturn"), 1)
                for c in range(2):
                    for e in range(4):
                        mm = pe.transpose(bank[1 + c][:, e * P:(e + 1) * P], vTh[:, e, c * P:(c + 1) * P], C("ident"))
                    mm.then_inc(S("r_vturn"), 1)
                for c in range(2):
                    for dt in range(2):
                        mm = pe.matmul(bank[3][:, c * P:(c + 1) * P], kTh[:, dt, c * P:(c + 1) * P],
                                       qTh[:, dt, c * P:(c + 1) * P], start=(dt == 0), stop=(dt == 1))
                mm.then_inc(S("r_scores"), 1)
                g = slice(32 * h, 32 * h + 32)
                for dt in range(2):
                    mm = pe.matmul(bank[4][g, dt * P:(dt + 1) * P], kTh[:, dt, dec], C("ident"), start=True, stop=True,
                                   skip_group_check=True)
                for dt in range(2):
                    mm = pe.matmul(bank[4][g, 256:288], kTh[:, dt, dec], qTh[:, dt, dec], start=(dt == 0),
                                   stop=(dt == 1), skip_group_check=True)
                mm.then_inc(S("r_dec"), 1)
                for e in range(4):
                    mm = pe.matmul(bank[5][g, e * P:(e + 1) * P], vTh[:, e, dec], C("ident"), start=True, stop=True,
                                   skip_group_check=True)
                mm.then_inc(S("r_dec"), 1)
                pe.wait_ge(S("r_ktail"), h + 1)
                pe.wait_ge(S("r_vtok"), 2 * h + 2)
                for dt in range(2):
                    mm = pe.matmul(bank[6 + dt][:, :], ktail[:, 0, dt * P:(dt + 1) * P], vtok[:, 0, :],
                                   start=True, stop=True)
                    mm.then_inc(S("r_s1"), 1)
                pe.wait_ge(S("r_st"), h + 1)
                pe.matmul(bank[0][:, :], ST[:, 0, :], vtok[:, 0, :], start=True, stop=True).then_inc(S("r_o"), 1)
                pe.matmul(bank[1][:, :], ST[:, 1, :], vtok[:, 1, :], start=True, stop=False)
                pe.wait_ge(S("r_s1out"), 2 * h + 2)
                for dt in range(2):
                    mm = pe.matmul(bank[1][:, :], qin[:, dt, :], s1[:, dt, :], start=False, stop=(dt == 1))
                mm.then_inc(S("r_o"), 1)
                for dt in range(2):
                    mm = pe.matmul(bank[6 + dt][:, :], ktail[:, 1, dt * P:(dt + 1) * P], vtok[:, 1, :],
                                   start=True, stop=True)
                    mm.then_inc(S("r_s2"), 1)

            def turn_outputs(h):
                for c in range(2):
                    pe.wait_ge(S("r_normed"), 2 * h + c + 1)
                    for e in range(4):
                        mm = pe.transpose(bank[2 + c][:, e * P:(e + 1) * P], on[:, c, e * P:(e + 1) * P], C("ident"))
                    mm.then_inc(S("r_oturn"), 1)

            for h in range(H):
                if h == 0:
                    project_in("rin", 0, hT, ret_drained, normed=NORM_DONE["mix1"])
                for c in (3 * h + 1, 3 * h + 2):
                    project_in("rin", c, hT, ret_drained)
                retention(h)
                if h < H - 1:
                    pe.wait_ge(S("r_decout_a"), h + 1)
                    pe.wait_ge(S("r_var"), 2 * h + 1)
                    project_in("rin", 3 * h + 3, hT, ret_drained, lambda: pe.wait_ge(S("r_s2out"), 2 * h + 2))
                turn_outputs(h)
                pe.wait_ge(S("r_head"), h + 1)
            pe.wait_ge(S("r_decout_a"), H)
            pe.matmul(bank[0][:, :], STd, vdec, start=True, stop=False, skip_group_check=True)
            pe.wait_ge(S("qmask_r"), 4)
            for b in range(NB):
                st = landed(pe, ("st", b)).rearrange("p (h n) -> p h n", h=8)
                for dt in range(2):
                    for h in range(H):
                        mm = pe.matmul(bank[0][32 * h:32 * h + 32, :], qm[:, 2 * h + dt, 32 * b:32 * b + 32],
                                       st[:, 2 * h + dt, :], start=False, stop=(b == NB - 1 and dt == 1),
                                       skip_group_check=True)
                mm.then_inc(S("d_cross"), 1)
                for h in range(H):
                    n = b * H + h
                    if h == 1 and b - 1 in QUERY_AFTER:
                        pe.wait_ge(S("rin_out_a"), QUERY_AFTER[b - 1] + 1)
                    pe.wait_ge(S("kvar_ready"), n + 1)
                    for dt in range(2):
                        q = 2 * n + dt
                        if q >= 4:
                            pe.wait_ge(S("d_state"), q - 3)
                        mm = pe.matmul(bank[1 + q % 4][:, :], kvar[n % 2][:, dt * P:(dt + 1) * P], vdec,
                                       start=True, stop=True)
                        mm.then_inc(S("d_add"), 1)
                if b in QUERY_AFTER:
                    c = QUERY_AFTER[b]
                    project_in("rin", c, hT, lambda c: pe.wait_ge(S("d_state"), 8 * b + 8))
            pe.wait_ge(S("r_normed"), 9)
            pe.wait_ge(S("d_state"), 64)
            for e in range(4):
                mm = pe.transpose(bank[2][:, e * P:(e + 1) * P], on[:, 0, e * P:(e + 1) * P], C("ident"))
            mm.then_inc(S("r_oturn"), 1)
            pe.wait_ge(S("d_out"), 1)
            attention(1)
            project_out(1, 24)
            pe.wait_ge(S("ms_out"), 5)
            route(1)
            experts(1, OFF_M1)
            combine(1)
            norm_sum("final", T)

        @block.scalar
        def _(act):
            def squares(name, src, n, ready):
                if NORM[name]:
                    act.wait_ge(S("sumsq"), NORM[name])
                for k in range(KD):
                    ready(k)
                    act.activation(sq[:, k, 0:n], src[:, k, :], ACT.Square).then_inc(S("squared"), 1)
                act.wait_ge(S("sumsq"), NORM[name] + 1)
                if NORM[name]:
                    act.wait_ge(S("normed"), NORM_DONE[name] - (16 if name == "mem" else 8))
                act.activation(ms[:, 0:n], bank[7][:, 0:n], ACT.Sqrt, scale=1.0 / D, bias=C("eps")) \
                   .then_inc(S("ms_out"), 1)

            def memory_kv():
                for j in range(4):
                    act.wait_ge(S("kv_sum"), j + 1)
                    act.activation(Ktok[:, j % 2, (j // 2) * 512:(j // 2 + 1) * 512], bank[j][:, :], ACT.Copy) \
                       .then_inc(S("ktok_out"), 1)
                for g in (1, 3):
                    act.wait_ge(S("kt_turned"), g + 1)
                    act.activation(KT[:, 2 * g:2 * g + 2, :], v3(bank[g][:, :], 2), ACT.Copy) \
                       .then_inc(S("kt_out_a"), 1)

            def keys_ahead():
                for j in range(4):
                    act.wait_ge(S("kv_sum"), 8 + j + 1)
                    act.activation(keys1[:, j % 2, (j // 2) * 512:(j // 2 + 1) * 512],
                                   bank[(4, 7, 0, 1)[j]][:, :], ACT.Copy).then_inc(S("kv1_out"), 1)
                act.wait_ge(S("kv1_out"), 4)
                act.dma_start(a["out_mk"][1].rearrange("(m p) n -> p m n", p=P), keys1) \
                    .then_inc(S("keys_stored1"), 16)

            def values_ahead():
                for j in range(4):
                    act.wait_ge(S("kv_sum"), 12 + j + 1)
                    act.activation(V[:, j % 2, (j // 2) * 512:(j // 2 + 1) * 512],
                                   bank[(4, 7, 5, 6)[j]][:, :], ACT.Copy).then_inc(S("values1_out"), 1)
                act.wait_ge(S("values1_out"), 4)
                act.dma_start(a["out_mv"][1].rearrange("(m p) n -> p m n", p=P), V) \
                    .then_inc(S("values_stored1"), 16)

            def store_state(b):
                act.wait_ge(S("d_state"), 8 * (b + 1))
                if b >= 2:
                    act.wait_ge(S(f"state_stored{b % 2}"), 16 * (b // 2))
                act.dma_start(a["out_rs"][b], slot(part(("st", b))[2]).rearrange("p (h n) -> p h n", h=8)) \
                    .then_inc(S(f"state_stored{b % 2}"), 16)

            def keys_turned():
                for g in range(4):
                    act.wait_ge(S("kt_turned"), 4 + g + 1)
                    act.activation(KT[:, 2 * g:2 * g + 2, :], v3(bank[(4, 5, 6, 0)[g]][:, :], 2), ACT.Copy) \
                       .then_inc(S("kt_out_a"), 1)

            def attention(i):
                act.wait_ge(S("normed"), NORM_DONE[f"mix{i}"])
                for j in range(9):
                    act.wait_ge(S("neg_max"), 9 * i + j + 1)
                    if j >= 2:
                        act.wait_ge(S("p_turned"), 9 * i + j - 1)
                    src = bank[0] if j == 0 else bank[1 + (j - 1) % 2]
                    act.activation(Pm[j % 2], src[:, 0:NM], ACT.Exp, bias=nb_[:, j:j + 1], scale=1.0 / 16,
                                   accum_out=rs[:, j:j + 1]).then_inc(S("exp_done"), 1)
                    if j >= 2:
                        turned(i, j - 1)
                turned(i, 8)
                act.wait_ge(S("dec_pv"), 4 * i + 4)
                act.activation(od, bank[7][:, 0:NM], ACT.Copy).then_inc(S("od_out"), 1)

            def turned(i, j):
                h, tb = divmod(j - 1, 2)
                act.wait_ge(S("p_turned"), 9 * i + j + 1)
                if h >= 2:
                    act.wait_ge(S("pv_sum"), 4 * i + h - 1)
                act.activation(PT[h % 2][:, :, tb * P:(tb + 1) * P], v3(bank[3 + j % 2][:, 0:256], 2), ACT.Copy) \
                   .then_inc(S("pt_out"), 1)

            def route(i):
                for j in range(6):
                    b, half = divmod(j, 2)
                    n = BLK[b][1]
                    act.wait_ge(S("h_turned"), 6 * i + j + 1)
                    act.activation(htok[b][0:n, half * 512:(half + 1) * 512], bank[j % 4][0:n, :], ACT.Copy) \
                       .then_inc(S("htok_out"), 1)
                act.activation(small[:, 72:73], C("eps"), ACT.Copy).then_inc(S(f"y_out_a{i}"), 1)
                act.wait_ge(S("g_max"), i + 1)
                for b in range(3):
                    act.activation(g4[:, b, :], rl[:, b, 0:NG], ACT.Exp, bias=ng[:, b:b + 1],
                                   accum_out=gs[:, b:b + 1]).then_inc(S("g_exp"), 1)
                act.wait_ge(S("e_max"), i + 1)
                for b in range(3):
                    act.activation(e8[:, b, :], em8[:, b, :], ACT.Exp, bias=ne[:, b:b + 1],
                                   accum_out=es[:, b:b + 1]).then_inc(S("e_exp"), 1)

            def experts(L):
                act.wait_ge(S(f"values_stored{L}"), 16)
                act.wait_ge(S(f"npass{L}"), 1)
                npr = act.value_load(npass[0:1, L:L + 1], min_val=0, max_val=PASSES - 1) + 1

                def picked_out(it, u):
                    act.wait_ge(S(f"x_picked{L}"), 4 * it + (2 * u + 1))
                    act.activation(xgT[u][:, 0:4, :], v3(bank[0][:, :], 4), ACT.Copy).then_inc(S(f"xt_out_a{L}"), 1)

                def pair(p, i, u, more):
                    it = p * (PAIRS // 2) + i
                    g = 2 * it + u
                    act.wait_ge(S(f"gu_sum{L}"), g + 1)
                    act.activation(tg[u], bank[2 + u][:, 0:FF], ACT.Tanh, scale=0.5).then_inc(S(f"tanh{L}"), 1)
                    if more:
                        picked_out(it + u, 1 - u)
                    act.wait_ge(S(f"y_sum{L}"), 2 * g + 1)
                    act.wait_ge(S(f"scattered{L}"), 16 * g + 16)
                    act.activation(yo[u][:, 0:512], bank[5][:, :], ACT.Copy).then_inc(S(f"y_out_a{L}"), 1)

                with act.Fori(0, npr) as p:
                    picked_out(p * (PAIRS // 2), 0)
                    with act.Fori(0, PAIRS // 2 - 1) as i:
                        pair(p, i, 0, True)
                        pair(p, i, 1, True)
                    pair(p, PAIRS // 2 - 1, 0, True)
                    pair(p, PAIRS // 2 - 1, 1, False)

            act.wait_ge(S("const_in"), 32)
            act.wait_ge(S("mem_in"), 16)
            squares("mem", memT, NM, lambda k: None)
            act.wait_ge(S("x_in"), 16)
            squares("mix0", xT, T, lambda k: None)
            memory_kv()
            for c in range(8):
                act.wait_ge(S("cin_sum"), 4 * c + 1)
                if c >= 2:
                    act.wait_ge(S("conv_out"), c - 1)
                act.activation(c_sb[c % 2], bank[4 * (c % 2)][:, 0:T], ACT.Copy).then_inc(S("c_out"), 1)
                act.wait_ge(S("cin_sum"), 4 * c + 4)
                if c == 0:
                    act.wait_ge(S("keys_stored0"), 16)
                act.activation(qx[:, c, :], bank[4 * (c % 2) + 3][:, 0:T], ACT.Copy).then_inc(S("qx_out0"), 1)
            attention(0)
            squares("ffn0", xT, T, lambda k: act.wait_ge(S("res_add"), k + 1))
            route(0)
            keys_ahead()
            experts(0)
            values_ahead()
            squares("mix1", xT, T, lambda k: act.wait_ge(S("moe_add"), 6))
            keys_turned()
            for c in range(12):
                kind, h = c % 3, c // 3
                for o in range(4):
                    act.wait_ge(S("rin_sum"), 4 * c + o + 1)
                    bk = rin_banks(c)[o]
                    if kind == 1:
                        ins = act.activation(vTh[:, o, :], bk, ACT.Copy)
                    elif kind == 2:
                        if 4 * h + o >= 2:
                            act.wait_ge(S("r_gate"), 4 * h + o - 1)
                        act.activation(th[o % 2], bk, ACT.Tanh, scale=0.5).then_inc(S("r_tanh"), 1)
                        ins = act.activation(cat[:, 4 * h + o, :], bk, ACT.Copy,
                                             scale=G("gn")[:, 4 * h + o:4 * h + o + 1])
                        if o < 3:
                            ins.then_inc(S("r_gg"), 1)
                if kind == 0:
                    act.nop().then_inc(S("rin_out_a"), 1)
                elif kind == 1:
                    ins.then_inc(S("rin_out_a"), 1)
                else:
                    ins.then_inc(S("r_gg"), 1)
                    act.wait_ge(S("r_gg"), 4 * h + 4)
                    act.nop().then_inc(S("rin_out_a"), 1)
                    for q in range(2):
                        act.wait_ge(S("r_vturn"), 2 * h + q + 1)
                        act.activation(vtok[:, q, :], bank[1 + q][:, :], ACT.Copy).then_inc(S("r_vtok"), 1)
                    g = slice(32 * h, 32 * h + 32)
                    act.wait_ge(S("r_dec"), 2 * h + 2)
                    act.activation(vdec[g, :], bank[5][g, :], ACT.Copy).then_inc(S("r_decout_a"), 1)
                    for dt in range(2):
                        act.wait_ge(S("r_s1"), 2 * h + dt + 1)
                        if h and dt == 0:
                            act.wait_ge(S("ret_stored"), 16 * h)
                        act.activation(s1[:, dt, :], bank[6 + dt][:, :], ACT.Copy).then_inc(S("r_s1out"), 1)
            for b in range(NB):
                store_state(b)
                if b in QUERY_AFTER:
                    c = QUERY_AFTER[b]
                    for o in range(4):
                        act.wait_ge(S("rin_sum"), 4 * c + o + 1)
                        ins = act.activation(qx[:, 4 * (c - 12) + o, :], rin_banks(c)[o], ACT.Copy)
                    ins.then_inc(S("rin_out_a"), 1)
            attention(1)
            squares("ffn1", xT, T, lambda k: act.wait_ge(S("res_add"), 8 + k + 1))
            route(1)
            experts(1)
            squares("final", xT, T, lambda k: act.wait_ge(S("moe_add"), 12))

        @block.vector
        def _(dve):
            def V_(ins):
                chain(dve, "vector_chain", ins)

            def norm(name, src, dests, n):
                dve.wait_ge(S("ms_out"), NORM[name] + 1)
                V_(dve.reciprocal(rstd[:, 0:n], ms[:, 0:n]))
                for dst, gname in dests:
                    for k in range(KD):
                        dve.scalar_tensor_tensor(out=dst[:, k, :], in0=src[:, k, :], scalar=G(gname)[:, k:k + 1],
                                                 in1=rstd[:, 0:n], op0=ALU.mult, op1=ALU.mult) \
                           .then_inc(S("normed"), 1)

            def memory_kv():
                for j in range(4, 8):
                    dve.wait_ge(S("kv_sum"), j + 1)
                    dve.tensor_copy(V[:, j % 2, (j // 2 - 2) * 512:(j // 2 - 1) * 512], bank[j][:, :]) \
                       .then_inc(S("v_out"), 1)
                for g in (0, 2):
                    dve.wait_ge(S("kt_turned"), g + 1)
                    dve.tensor_copy(KT[:, 2 * g:2 * g + 2, :], v3(bank[g][:, :], 2)).then_inc(S("kt_out_d"), 1)

            def attention(i, xo):
                qd = qx[:, :, TP:T].rearrange("p h (b s) -> p h b s", s=NS)
                dve.tensor_copy(qm_diag, qd).then_inc(S("qmask_x"), 1)

                def maximum(j):
                    if j == 0:
                        dve.wait_ge(S("dec_scores"), 4 * i + 4)
                    else:
                        dve.wait_ge(S("pr_scores"), 8 * i + j)
                    src = bank[0] if j == 0 else bank[1 + (j - 1) % 2]
                    V_(dve.tensor_reduce(mx[:, j:j + 1], src[:, 0:NM], AX.X, ALU.max))
                    dve.tensor_scalar(nb_[:, j:j + 1], mx[:, j:j + 1], -1.0 / 16, None, ALU.mult) \
                       .then_inc(S("neg_max"), 1)

                def normalise(j):
                    dve.wait_ge(S("exp_done"), 9 * i + j + 1)
                    V_(dve.reciprocal(rr[:, j:j + 1], rs[:, j:j + 1]))
                    dve.tensor_scalar(Pm[j % 2], Pm[j % 2], rr[:, j:j + 1], None, ALU.mult).then_inc(S("p_ready"), 1)

                def pv_out(h):
                    dve.wait_ge(S("pv_sum"), 4 * i + h + 1)
                    dve.tensor_copy(cat[:, xo + 2 * h:xo + 2 * h + 2, 0:TP], v3(bank[5 + h % 2][:, :], 2)) \
                       .then_inc(S("pv_out"), 1)

                maximum(0)
                for j in range(9):
                    if j + 1 < 9:
                        maximum(j + 1)
                    normalise(j)
                    if j == 0:
                        dve.wait_ge(S("p_turned"), 9 * i + 1)
                        for mb in range(2):
                            ins = dve.tensor_copy(qm_diag[:, 4 * mb:4 * mb + 4],
                                                  bank[3][:, mb * P:(mb + 1) * P]
                                                  .rearrange("p (h b s) -> p h b s", h=H, b=NB))
                            if mb == 0:
                                V_(ins)
                        ins.then_inc(S("pt0_out"), 1)
                    if j >= 6 and j % 2 == 0:
                        pv_out((j - 6) // 2)
                pv_out(2)
                pv_out(3)
                dve.wait_ge(S("od_turned"), i + 1)
                for dt in range(2):
                    ins = dve.tensor_copy(cat[:, xo:xo + 8, TP:T].rearrange("p (h d) t -> p h d t", d=2)[:, :, dt, :],
                                          bank[0][:, dt * P:(dt + 1) * P].rearrange("p (h t) -> p h t", h=H))
                    if dt == 0:
                        V_(ins)
                ins.then_inc(S("cat_out"), 1)
                dve.wait_ge(S("cat_out"), i + 1)
                dve.wait_ge(S("pv_out"), 4 * i + 4)
                dve.nop().then_inc(S("cat_ready"), 1)

            def residual(i):
                for o in range(KD):
                    dve.wait_ge(S("proj"), 8 * i + o + 1)
                    dve.tensor_tensor(xT[:, o, :], xT[:, o, :], bank[1 + o % 4][:, 0:T], ALU.add) \
                       .then_inc(S("res_add"), 1)

            def route(i):
                V_(dve.memset(rl, 0.0))
                V_(dve.memset(lgp, -BIG))
                dve.wait_ge(S("logits"), i + 1)
                V_(dve.tensor_copy(rl[:, 0:2, :], v3(bank[6][:, 0:72], 2)))
                V_(dve.tensor_copy(rl[0:32, 2, :], bank[6][0:32, 72:108]))
                V_(dve.tensor_copy(lgp[:, :, 0:NG], rl[:, :, 0:NG]))
                for b in range(3):
                    V_(dve.max(gm8[:, b, :], lgp[:, b, :]))
                    V_(dve.max_index(gi8[:, b, :], gm8[:, b, :], lgp[:, b, :]))
                dve.tensor_scalar(ng, gm8[:, :, 0], -1.0, None, ALU.mult).then_inc(S("g_max"), 1)
                V_(dve.tensor_copy(gf, gi8[:, :, 0]))
                V_(dve.tensor_tensor(pen, C("iota")[:, 0:NG].unsqueeze(1).to_broadcast([P, 3, NG]),
                                     gf.unsqueeze(2).to_broadcast([P, 3, NG]), ALU.is_equal))
                V_(dve.tensor_scalar(pen, pen, -1.0, BIG, ALU.add, ALU.mult))
                for b in range(3):
                    V_(dve.tensor_tensor(lem[:, b], rl[:, b, NG:].rearrange("p (g e) -> p g e", g=NG),
                                         pen[:, b, :].unsqueeze(2).to_broadcast([P, NG, EPG]), ALU.add))
                lemf = lem.rearrange("p b g e -> p b (g e)")
                for b in range(3):
                    V_(dve.max(em8[:, b, :], lemf[:, b, :]))
                    V_(dve.max_index(ei8[:, b, :], em8[:, b, :], lemf[:, b, :]))
                dve.tensor_scalar(ne, em8[:, :, 0], -1.0, None, ALU.mult).then_inc(S("e_max"), 1)
                V_(dve.tensor_copy(ef, ei8[:, :, 0:2]))
                for k in range(2):
                    V_(dve.tensor_tensor(oh[:, :, k, :], C("iota").unsqueeze(1).to_broadcast([P, 3, NE]),
                                         ef[:, :, k].unsqueeze(2).to_broadcast([P, 3, NE]), ALU.is_equal))
                V_(dve.tensor_tensor(M, oh[:, :, 0, :], oh[:, :, 1, :], ALU.add))
                dve.tensor_tensor(M, M, C("valid").unsqueeze(2).to_broadcast([P, 3, NE]), ALU.mult) \
                   .then_inc(S("chosen"), 1)
                dve.wait_ge(S("e_exp"), 3 * i + 3)
                dve.wait_ge(S("g_exp"), 3 * i + 3)
                V_(dve.reciprocal(es, es))
                V_(dve.tensor_tensor(pe2, e8[:, :, 0:2], es.unsqueeze(2).to_broadcast([P, 3, 2]), ALU.mult))
                V_(dve.tensor_tensor(fr, pe2[:, :, 0], pe2[:, :, 1], ALU.add))
                V_(dve.tensor_tensor(fr, fr, gs, ALU.mult))
                V_(dve.reciprocal(fr, fr))
                V_(dve.tensor_scalar(fr, fr, 0.5, None, ALU.mult))
                V_(dve.tensor_tensor(pe2, pe2, fr.unsqueeze(2).to_broadcast([P, 3, 2]), ALU.mult))
                ci = cst[:, :].bitcast(I32)
                pr = CC["pair"][0]
                V_(dve.tensor_copy(rec_gate, pe2))
                V_(dve.tensor_copy(rec[:, :, :, 0], ci[:, pr:pr + 6].rearrange("p (b k) -> p b k", b=3)))
                dve.wait_ge(S("ranks"), i + 1)
                dve.memset(small[:, 73:74], 0.0).then_inc(S(f"y_out_d{i}"), 1)
                V_(dve.memset(rk_, 0.0))
                dve.scalar_tensor_tensor(out=rk[:, :, 0:NE], in0=v3(bank[5][:, 0:96], 3), scalar=1.0, in1=M,
                                         op0=ALU.add, op1=ALU.mult).then_inc(S(f"slots_known{i}"), 1)
                V_(dve.scalar_tensor_tensor(out=Gx, in0=v3(bank[5][:, 0:96], 3), scalar=float(PAIRS),
                                            in1=C("cexp").unsqueeze(1).to_broadcast([P, 3, NE]),
                                            op0=ALU.mult, op1=ALU.add))
                for k in range(2):
                    V_(dve.tensor_tensor(prod[:, :, k, :], oh[:, :, k, :], Gx, ALU.mult))
                V_(dve.tensor_reduce(idxf, prod, AX.X, ALU.add))
                V_(dve.tensor_tensor(idxf, idxf, C("far").unsqueeze(2).to_broadcast([P, 3, 2]), ALU.add))
                dve.tensor_copy(idxi, idxf).then_inc(S("places"), 1)
                V_(dve.tensor_reduce(cmx[0:1, :], bank[5][0:1, 96:128], AX.X, ALU.max))
                V_(dve.tensor_scalar(cgt[0:1, :], C("thr")[0:1, :], cmx[0:1, 0:1], None, ALU.is_lt))
                V_(dve.tensor_reduce(npf[0:1, :], cgt[0:1, :], AX.X, ALU.add))
                dve.tensor_copy(npass[0:1, i:i + 1], npf[0:1, :]).then_inc(S(f"npass{i}"), 1)

            def experts(L):
                dve.wait_ge(S(f"values_stored{L}"), 16)

                def select(u, e):
                    dve.tensor_tensor(onehot[u].rearrange("p b (c s) -> p b c s", c=2),
                                      C("slots").unsqueeze(1).unsqueeze(1).to_broadcast([P, 3, 2, CAP]),
                                      rk[:, :, bass.ds(e, 2)].unsqueeze(3).to_broadcast([P, 3, 2, CAP]),
                                      ALU.is_equal).then_inc(S(f"selected{L}"), 1)

                dve.wait_ge(S(f"npass{L}"), 1)
                npr = dve.value_load(npass[0:1, L:L + 1], min_val=0, max_val=PASSES - 1) + 1

                def picked_out(it, u):
                    dve.wait_ge(S(f"x_picked{L}"), 4 * it + (2 * u + 2))
                    dve.tensor_copy(xgT[u][:, 4:8, :], v3(bank[1][:, :], 4)).then_inc(S(f"xt_out_d{L}"), 1)

                def pair(p, i, u, more):
                    it = p * (PAIRS // 2) + i
                    g = 2 * it + u
                    dve.wait_ge(S(f"tanh{L}"), g + 1)
                    dve.scalar_tensor_tensor(out=tg[u], in0=tg[u], scalar=1.0, in1=bank[2 + u][:, 0:FF],
                                             op0=ALU.add, op1=ALU.mult).then_inc(S(f"silu{L}"), 1)
                    dve.wait_ge(S(f"silu{L}"), g + 1)
                    dve.wait_ge(S(f"gates{L}{u}"), it + p + 1)
                    dve.scalar_tensor_tensor(out=act_[u], in0=tg[u], scalar=gate_c[u],
                                             in1=bank[2 + u][:, FF:2 * FF], op0=ALU.mult, op1=ALU.mult) \
                       .then_inc(S(f"act_ready{L}"), 1)
                    if more:
                        picked_out(it + u, 1 - u)
                    dve.wait_ge(S(f"act_turned{L}"), g + 1)
                    dve.tensor_copy(actT[u], v3(bank[4][:, 0:256], 2)).then_inc(S(f"actT_out{L}"), 1)
                    select(u, i * 4 + (2 * u + 4))
                    dve.wait_ge(S(f"y_sum{L}"), 2 * g + 2)
                    dve.wait_ge(S(f"scattered{L}"), 16 * g + 16)
                    dve.tensor_copy(yo[u][:, 512:1024], bank[6][:, :]).then_inc(S(f"y_out_d{L}"), 1)

                with dve.Fori(0, npr) as p:
                    dve.wait_ge(S(f"slots_known{L}"), p + 1)
                    select(0, 0)
                    select(1, 2)
                    picked_out(p * (PAIRS // 2), 0)
                    with dve.Fori(0, PAIRS // 2 - 1) as i:
                        pair(p, i, 0, True)
                        pair(p, i, 1, True)
                    pair(p, PAIRS // 2 - 1, 0, True)
                    pair(p, PAIRS // 2 - 1, 1, False)
                    dve.wait_ge(S(f"selected{L}"), p * (PAIRS + 2) + (PAIRS + 2))
                    dve.tensor_scalar(rk_, rk_, -float(CAP), None, ALU.add).then_inc(S(f"slots_known{L}"), 1)

            def combine(L):
                for b, (t0, n) in enumerate(BLK):
                    dve.wait_ge(S(f"rows_in{b}"), 16 * (L + 1))
                    dve.tensor_tensor(yl[b][0:n, 0:D], yl[b][0:n, 0:D], yl[b][0:n, D:2 * D], ALU.add) \
                       .then_inc(S("rows_added"), 1)
                for j in range(6):
                    b, half = divmod(j, 2)
                    t0, n = BLK[b]
                    dve.wait_ge(S("rows_turned"), 6 * L + j + 1)
                    dst = xT[:, 4 * half:4 * half + 4, t0:t0 + n]
                    dve.tensor_tensor(dst, dst, v3(bank[j % 4][:, :], 4)[:, :, 0:n], ALU.add) \
                       .then_inc(S("moe_add"), 1)

            def group_norm(src, dst, ready, n):
                ready()
                V_(dve.bn_stats(bn6[:, 0:6], src[:, :]))
                V_(dve.bn_aggr(mv[:, 0:2], bn6[:, 0:6]))
                dve.tensor_scalar(mv[:, 1:2], mv[:, 1:2], EPS, None, ALU.add).then_inc(S("r_var"), 1)
                dve.wait_ge(S("r_pow"), n + 1)
                V_(dve.tensor_scalar(gv[:, 1:2], gv[:, 0:1], 0.5, None, ALU.mult))
                dve.tensor_scalar(dst, src[:, :], mv[:, 0:1], gv[:, 1:2], ALU.subtract, ALU.mult) \
                   .then_inc(S("r_normed"), 1)

            dve.wait_ge(S("const_in"), 32)
            dve.wait_ge(S("mem_in"), 16)
            norm("mem", memT, ((hm0, "mem0"), (hm1, "mem1")), NM)
            dve.wait_ge(S("x_in"), 16)
            norm("mix0", xT, ((hT, "mix0"),), T)
            memory_kv()
            V_(dve.memset(qm_, 0.0))
            for c in range(8):
                bk = [bank[4 * (c % 2) + o][:, 0:T] for o in range(4)]
                f, y = full[c % 2], yc[c % 2]
                fd = f[:, 258:306].rearrange("p (b t) -> p b t", b=NB)
                yd = y[:, TP:T].rearrange("p (b t) -> p b t", b=NB)
                if c == 0:
                    dve.wait_ge(S("states_in"), 16)
                dve.memset(f[:, 0:2], 0.0)
                dve.tensor_copy(fd[:, :, 0:2], stc[:, c, :].rearrange("p (b t) -> p b t", b=NB))
                dve.wait_ge(S("c_out"), c + 1)
                dve.wait_ge(S("cin_sum"), 4 * c + 2)
                dve.tensor_tensor(f[:, 2:258], c_sb[c % 2][:, 0:TP], bk[1][:, 0:TP], ALU.mult)
                V_(dve.tensor_tensor(fd[:, :, 2:6], c_sb[c % 2][:, TP:T].rearrange("p (b t) -> p b t", b=NB),
                                     bk[1][:, TP:T].rearrange("p (b t) -> p b t", b=NB), ALU.mult))
                w = G("cw")[:, 3 * c:3 * c + 3]
                dve.tensor_scalar(y[:, 0:TP], f[:, 0:TP], w[:, 0:1], None, ALU.mult)
                V_(dve.tensor_scalar(yd, fd[:, :, 0:4], w[:, 0:1], None, ALU.mult))
                for q in (1, 2):
                    dve.scalar_tensor_tensor(out=y[:, 0:TP], in0=f[:, q:TP + q], scalar=w[:, q:q + 1],
                                             in1=y[:, 0:TP], op0=ALU.mult, op1=ALU.add)
                    V_(dve.scalar_tensor_tensor(out=yd, in0=fd[:, :, q:q + 4], scalar=w[:, q:q + 1], in1=yd,
                                                op0=ALU.mult, op1=ALU.add))
                dve.tensor_copy(cvp[:, c, :], f[:, 256:258])
                dve.tensor_copy(cvs[:, c, :].rearrange("p (b t) -> p b t", b=NB), fd[:, :, 4:6])
                dve.wait_ge(S("cin_sum"), 4 * c + 3)
                dve.tensor_tensor(cat[:, c, :], y, bk[2], ALU.mult).then_inc(S("conv_out"), 1)
            dve.wait_ge(S("conv_out"), 8)
            dve.wait_ge(S("qx_out0"), 8)
            attention(0, 8)
            residual(0)
            norm("ffn0", xT, ((hT, "ffn0"),), T)
            route(0)
            experts(0)
            combine(0)
            dve.wait_ge(S("keys_stored1"), 16)
            norm("mix1", xT, ((hT, "mix1"),), T)
            V_(dve.memset(STd, 0.0))
            cos, sin = C("cos"), C("sin")
            for c in range(12):
                kind, h = c % 3, c // 3
                g = slice(32 * h, 32 * h + 32)
                bk = rin_banks(c)
                if kind == 0:
                    for n, dst in ((0, qTh), (2, kTh)):
                        dve.wait_ge(S("rin_sum"), 4 * c + n + 2)
                        V_(dve.tensor_tensor(dst[:, 0, :], bk[n], cos, ALU.mult))
                        V_(dve.tensor_tensor(rot, bk[n + 1], sin, ALU.mult))
                        V_(dve.tensor_tensor(dst[:, 0, :], dst[:, 0, :], rot, ALU.subtract))
                        V_(dve.tensor_tensor(dst[:, 1, :], bk[n], sin, ALU.mult))
                        V_(dve.tensor_tensor(rot, bk[n + 1], cos, ALU.mult))
                        V_(dve.tensor_tensor(dst[:, 1, :], dst[:, 1, :], rot, ALU.add))
                    inner = C("inner")[:, h * P:(h + 1) * P]
                    dve.tensor_tensor(qin, qTh[:, :, P:2 * P], inner.unsqueeze(1).to_broadcast([P, 2, P]), ALU.mult)
                    for dt in range(2):
                        ins = dve.tensor_tensor(qm_diag[:, 2 * h + dt],
                                                qTh[:, dt, TP:T].rearrange("p (b s) -> p b s", s=NS),
                                                inner[:, 0:NS].unsqueeze(1).to_broadcast([P, NB, NS]), ALU.mult)
                        if dt == 0:
                            V_(ins)
                    ins.then_inc(S("qmask_r"), 1)
                    dve.wait_ge(S("qmask_r"), h + 1)
                    dve.nop().then_inc(S("rin_out"), 1)
                elif kind == 1:
                    dve.nop().then_inc(S("rin_out"), 1)
                else:
                    for o in range(4):
                        n = 4 * h + o
                        dve.wait_ge(S("r_tanh"), n + 1)
                        dve.wait_ge(S("r_gg"), n + 1)
                        dve.scalar_tensor_tensor(out=cat[:, n, :], in0=th[o % 2], scalar=1.0, in1=cat[:, n, :],
                                                 op0=ALU.add, op1=ALU.mult).then_inc(S("r_gate"), 1)
                    dve.wait_ge(S("r_gate"), 4 * h + 4)
                    dve.nop().then_inc(S("rin_out"), 1)
                    dve.wait_ge(S("r_kturn"), h + 1)
                    dve.tensor_scalar(ktail, v3(bank[0][:, :], 2), C("tail")[:, h:h + 1], None, ALU.mult) \
                       .then_inc(S("r_ktail"), 1)
                    dve.wait_ge(S("r_scores"), h + 1)
                    dve.tensor_tensor(ST, v3(bank[3][:, 0:256], 2),
                                      C("decay")[:, h * P:(h + 1) * P].unsqueeze(1).to_broadcast([P, 2, P]),
                                      ALU.mult).then_inc(S("r_st"), 1)
                    dve.wait_ge(S("r_dec"), 2 * h + 1)
                    V_(dve.tensor_scalar(kdec[g, :], bank[4][g, 0:256], C("tdec")[g, 0:1], None, ALU.mult))
                    V_(dve.tensor_tensor(STd[g, g], bank[4][g, 256:288], C("dmask")[g, :], ALU.mult))
                    for q in range(2):
                        group_norm(bank[q], on[:, q, :], lambda: dve.wait_ge(S("r_o"), 2 * h + q + 1), 2 * h + q)
                    for dt in range(2):
                        dve.wait_ge(S("r_s2"), 2 * h + dt + 1)
                        ins = dve.scalar_tensor_tensor(out=s1[:, dt, :], in0=s1[:, dt, :],
                                                       scalar=float(np.exp(P * LOGG[h])),
                                                       in1=bank[6 + dt][:, :], op0=ALU.mult, op1=ALU.add)
                        ins.then_inc(S("r_s2out"), 1)
                    for q in range(2):
                        dve.wait_ge(S("r_oturn"), 2 * h + q + 1)
                        dst = cat[:, 4 * h:4 * h + 4, q * P:(q + 1) * P]
                        ins = dve.tensor_tensor(dst, dst, v3(bank[2 + q][:, :], 4), ALU.mult)
                        if q == 0:
                            V_(ins)
                    ins.then_inc(S("r_head"), 1)
            for b in range(NB):
                st = slot(part(("st", b))[2]).rearrange("p (h n) -> p h n", h=8)
                landed(dve, ("st", b))
                dve.wait_ge(S("d_cross"), b + 1)
                if b == NB - 1:
                    group_norm(bank[0], on[:, 0, :], lambda: None, 8)
                for h in range(H):
                    for dt in range(2):
                        q = 8 * b + 2 * h + dt
                        dve.wait_ge(S("d_add"), q + 1)
                        dve.scalar_tensor_tensor(out=st[:, 2 * h + dt, :], in0=st[:, 2 * h + dt, :],
                                                 scalar=float(np.exp(NS * LOGG[h])), in1=bank[1 + q % 4][:, :],
                                                 op0=ALU.mult, op1=ALU.add).then_inc(S("d_state"), 1)
            dve.wait_ge(S("r_oturn"), 9)
            for e in range(4):
                dst = cat[:, 0:16, TP:T].rearrange("p (h e) t -> p h e t", e=4)[:, :, e, :]
                ins = dve.tensor_tensor(dst, dst, bank[2][:, e * P:(e + 1) * P].rearrange("p (h t) -> p h t", h=H),
                                        ALU.mult)
                if e < 3:
                    V_(ins)
            ins.then_inc(S("d_out"), 1)
            dve.wait_ge(S("rin_out_a"), 14)
            attention(1, 16)
            residual(1)
            norm("ffn1", xT, ((hT, "ffn1"),), T)
            route(1)
            experts(1)
            combine(1)
            norm("final", xT, ((hT, "final"),), T)

        @block.gpsimd
        def _(pool):
            def store_memory():
                pool.wait_ge(S("ktok_out"), 4)
                pool.dma_start(a["out_mk"][0].rearrange("(m p) n -> p m n", p=P), Ktok).then_inc(S("keys_stored0"), 16)
                pool.wait_ge(S("v_out"), 4)
                pool.dma_start(a["out_mv"][0].rearrange("(m p) n -> p m n", p=P), V).then_inc(S("values_stored0"), 16)

            def keys_back():
                pool.wait_ge(S("keys_stored1"), 16)
                pool.dma_start(Ktok, a["out_mk"][1].rearrange("(m p) n -> p m n", p=P)).then_inc(S("keys_back"), 16)

            def route(i):
                pool.wait_ge(S("cat_ready"), i + 1)
                pool.dma_start(wr_sb, a["wr"][i]).then_inc(S("router_in"), 16)
                for u in range(2):
                    pool.dma_start(Lt_[:, 2 * (PAIRS + u):2 * (PAIRS + u) + 2], a["lfill"][:, 0:2]) \
                        .then_inc(S(f"scattered{i}"), 16)
                    pool.wait_ge(S(f"scattered{i}"), 16 * u + 16)
                pool.wait_ge(S("places"), i + 1)
                pool.wait_ge(S("lists_filled"), 32)
                for b in range(3):
                    for k in range(2):
                        pool.indirect_dma_start(out=dram_l[i], out_offset=bass.IndirectOffsetOnAxis(
                            ap=idxi[:, b, k:k + 1].bitcast(U32), axis=0), in_=rec[:, b, k, :], in_offset=None,
                            bounds_check=2 * LROW - 1, oob_is_err=False).then_inc(S("listed"), 16)
                pool.wait_ge(S("listed"), 96 * (i + 1))

            def experts(L):
                def marked(i):
                    pool.tensor_tensor(flag[L][i], C("eps"), C("eps"), ALU.add).then_inc(S(f"picked{L}"), 1)

                pool.wait_ge(S(f"npass{L}"), 1)
                npr = pool.value_load(npass[0:1, L:L + 1], min_val=0, max_val=PASSES - 1) + 1
                with pool.Fori(0, npr) as p:
                    for half in range(2):
                        src = dram_l[L].rearrange("(h a) r -> h (a r)", h=2)[
                            half:half + 1, bass.ds(p * (CAP * PAIRS * 2), CAP * PAIRS * 2)]
                        pool.dma_start(Lt_[64 * half:64 * half + 64, 0:2 * PAIRS],
                                       src.rearrange("h (s n) -> (h s) n", s=CAP)).then_inc(S(f"list_in{L}"), 16)
                    pool.wait_ge(S(f"list_in{L}"), p * 32 + 32)
                    marked(4)

                    def gate(u, col):
                        pool.tensor_copy(gate_c[u].bitcast(I32), Lt_[:, bass.ds(col + 1, 1)]) \
                            .then_inc(S(f"gates{L}{u}"), 1)

                    per = 4 * PAIRS + 2
                    gate(0, 0)
                    gate(1, 2)
                    with pool.Fori(0, PAIRS // 2) as i:
                        it = p * (PAIRS // 2) + i
                        for u in range(2):
                            pool.wait_ge(S(f"act_ready{L}"), 2 * it + (u + 1))
                            marked(0)
                            gate(u, i * 4 + (2 * u + 4))
                            pool.wait_ge(S(f"scattered{L}"), 32 * it + (16 * u + 32))
                            marked(1)
                            pool.tensor_copy(pair_i[u], Lt_[:, bass.ds(i * 4 + 2 * u, 1)]) \
                                .then_inc(S(f"picked{L}"), 1)
                            pool.wait_ge(S(f"picked{L}"), per * p + i * 8 + (4 * u + 4))
                            pool.wait_ge(S(f"y_out_a{L}"), 2 * it + u + 2)
                            pool.wait_ge(S(f"y_out_d{L}"), 2 * it + u + 2)
                            marked(2)
                            pool.indirect_dma_start(out=dram_y[L], out_offset=bass.IndirectOffsetOnAxis(
                                ap=pair_i[u].bitcast(U32), axis=0), in_=yo[u], in_offset=None,
                                bounds_check=2 * T - 1, oob_is_err=False).then_inc(S(f"scattered{L}"), 16)
                    pool.wait_ge(S(f"slots_known{L}"), p + 2)
                    for u in range(2):
                        pool.wait_ge(S(f"gates{L}{u}"), p * (PAIRS // 2 + 1) + (PAIRS // 2 + 1))
                    pool.wait_ge(S(f"scattered{L}"), p * (16 * PAIRS) + (16 * PAIRS + 32))
                    marked(3)
                for b, (t0, n) in enumerate(BLK):
                    pool.dma_start(yl[b][0:n, :], dram_y[L][2 * t0:2 * (t0 + n), :]
                                   .rearrange("(t k) n -> t (k n)", k=2)).then_inc(S(f"rows_in{b}"), 16)

            pool.wait_ge(S("const_in"), 32)
            for i in range(2):
                pool.dma_start(dram_l[i].rearrange("(p a) r -> p (a r)", p=P), a["lfill"]) \
                    .then_inc(S("lists_filled"), 16)
            pool.dma_start(stc, a["stc"]).then_inc(S("states_in"), 16)
            store_memory()
            pool.wait_ge(S("conv_out"), 8)
            pool.dma_start(a["out_cvp"], cvp).then_inc(S("conv_stored"), 16)
            pool.dma_start(a["out_cvs"], cvs).then_inc(S("conv_stored"), 16)
            pool.wait_ge(S("conv_stored"), 32)
            route(0)
            experts(0)
            keys_back()
            for h in range(H):
                for q in range(2):
                    pool.wait_ge(S("r_var"), 2 * h + q + 1)
                    pool.tensor_tensor(gv[:, 0:1], mv[:, 1:2], C("neghalf"), ALU.pow).then_inc(S("r_pow"), 1)
                pool.wait_ge(S("r_s2out"), 2 * h + 2)
                pool.dma_start(a["out_rp"][h], s1).then_inc(S("ret_stored"), 16)
            for n in range(NB * H):
                if n >= 2:
                    pool.wait_ge(S("d_add"), 2 * (n - 1))
                if n == 0:
                    pool.wait_ge(S("r_head"), 4)
                pool.tensor_scalar(kvar[n % 2], kdec, C("kvmask")[:, n:n + 1], None, ALU.mult) \
                    .then_inc(S("kvar_ready"), 1)
                if n == NB * H - 3:
                    pool.wait_ge(S("r_var"), 9)
                    pool.tensor_tensor(gv[:, 0:1], mv[:, 1:2], C("neghalf"), ALU.pow).then_inc(S("r_pow"), 1)
            route(1)
            experts(1)
            for q in range(2):
                ks = slice(4 * q, 4 * q + 4)
                pool.wait_ge(S("normed"), NORM_DONE["final"] - 4 + 4 * q)
                pool.dma_start(a["out_y"][:, ks], hT[:, ks]).then_inc(S("y_stored"), 16)
            pool.wait_ge(S("y_stored"), 32)
            pool.wait_ge(S("conv_stored"), 32)
            pool.wait_ge(S("ret_stored"), 16 * H)
            for i in range(2):
                pool.wait_ge(S(f"keys_stored{i}"), 16)
                pool.wait_ge(S(f"values_stored{i}"), 16)
            for b in range(2):
                pool.wait_ge(S(f"state_stored{b}"), 16 * NB // 2)


OUTS = {"out_y": (P, KD, T), "out_cvp": (P, 8, 2), "out_cvs": (P, 8, 16), "out_rp": (H, P, 2, DV),
        "out_rs": (NB, P, 8, DV), "out_mk": (2, NM, D), "out_mv": (2, NM, D)}


def feature_major(v, k):
    return np.ascontiguousarray(v.reshape(-1, k, P).transpose(2, 1, 0))


def tiles(w, kt, per):
    n = w.shape[1] // P
    w = w.reshape(kt, P, n // per, per, P)
    return np.ascontiguousarray(w.transpose(2, 1, 3, 0, 4).reshape(n // per, P, per * kt * P))


def constants():
    f = np.float32
    c = np.zeros((P, NCC), f)

    def put(name, v):
        o, w = CC[name]
        c[:, o:o + w] = v

    i = np.arange(P)
    put("ident", np.eye(P))
    put("ones", 1.0)
    put("tri", (i[:, None] < i[None, :]))
    e = np.arange(NE)
    put("iota", e)
    put("cexp", (e % 2) * LROW + e // 2)
    pos = np.concatenate([np.arange(TP), np.tile(PAST + np.arange(NS), NB)]).astype(f)
    inv = np.power(f(10000.0), -np.arange(P, dtype=f) / f(P)).astype(f)
    ang = (pos[None, :] * inv[:, None]).astype(f).astype(np.float64)
    put("cos", np.cos(ang))
    put("sin", np.sin(ang))
    lg = np.array(LOGG)
    diff = i[None, :] - i[:, None]
    decay = np.where(diff >= 0, np.exp(np.maximum(diff, 0)[None] * lg[:, None, None]), 0.0) / 16.0
    put("decay", decay.transpose(1, 0, 2).reshape(P, -1))
    t = np.arange(TD)
    same = (t[:, None] // NS == t[None, :] // NS) & (t[None, :] >= t[:, None])
    dm = np.where(same, np.exp((t[None, :] - t[:, None])[None] * lg[:, None, None] * same), 0.0) / 16.0
    put("dmask", dm.reshape(P, TD))
    put("inner", np.exp((i + 1)[None, :] * lg[:, None]).reshape(1, -1))
    put("tail", np.exp((P - 1 - i)[:, None] * lg[None, :]) / 16.0)
    put("tdec", (np.exp((NS - 1 - t % NS)[None, :] * lg[:, None]) / 16.0).reshape(P, 1))
    h, b = i // TD, (i % TD) // NS
    n = np.arange(NB * H)
    put("kvmask", (b[:, None] == n[None, :] // H) & (h[:, None] == n[None, :] % H))
    put("neghalf", -0.5)
    put("eps", EPS)
    tok = np.arange(3)[None, :] * P + i[:, None]
    put("slots", 1 + np.arange(CAP))
    put("valid", tok < T)
    put("far", np.where(tok < T, 0, FAR))
    put("thr", CAP * np.arange(1, PASSES))
    o = CC["pair"][0]
    c.view(np.int32)[:, o:o + 6] = np.repeat(2 * tok, 2, 1) + np.tile([0, 1], 3)[None, :]
    return c


def lay_out(x):
    o = {"cst": constants()}
    o["xT"] = feature_major(np.concatenate([x["x_prompt"][0], x["x_sample"].reshape(TD, D)]), KD)
    o["memT"] = feature_major(x["mem_prompt"][0], KD)
    cols = [x["norm_mix"][0], x["norm_mix"][1], x["norm_ffn"][0], x["norm_ffn"][1], x["mem_norm"][0],
            x["mem_norm"][1], x["final_norm"], x["ret_gn"][0]]
    par = [c.reshape(-1, P).T for c in cols] + [x["conv_w"][0].reshape(3, 8, P).transpose(2, 1, 0).reshape(P, 24)]
    o["par"] = np.ascontiguousarray(np.concatenate(par, 1))
    o["wkv"] = np.ascontiguousarray(x["w_mem_kv"].reshape(2, KD, P, 4, 512).transpose(0, 3, 2, 1, 4)
                                    .reshape(8, P, SLOT))
    w = x["conv_w_in"][0].reshape(D, 4, 8, P)
    o["cin"] = tiles(w.transpose(0, 2, 1, 3)[:, :, [1, 2, 0, 3]].reshape(D, -1), KD, 4)
    o["cout"] = tiles(x["conv_w_out"][0], 16, 2)
    w = x["ret_w_in"][0]
    heads = []
    for h in range(H):
        heads += [w[:, 256 * h:256 * h + 256], w[:, 1024 + 256 * h:1280 + 256 * h],
                  w[:, 2048 + DV * h:2048 + DV * h + DV], w[:, 4096 + DV * h:4096 + DV * h + DV]]
    o["rin"] = tiles(np.concatenate(heads + [w[:, 6144:]], 1), KD, 4)
    o["rout"] = tiles(x["ret_w_out"][0], 24, 1)
    o["kc"] = np.ascontiguousarray(x["cache_mem_k"].reshape(2, 4, 2, NM, 8, P).transpose(0, 1, 5, 2, 4, 3)
                                   .reshape(8, P, SLOT))
    o["vc"] = np.ascontiguousarray(x["cache_mem_v"].reshape(2, 4, 2, 2, P, D).transpose(0, 1, 4, 2, 3, 5)
                                   .reshape(8, P, SLOT))
    o["st"] = np.ascontiguousarray(x["state_ret"][0].reshape(NB, H, 2, P, DV).transpose(0, 3, 1, 2, 4)
                                   .reshape(NB, P, SLOT))
    o["stc"] = np.ascontiguousarray(x["state_conv"][0].reshape(NB, 2, 8, P).transpose(3, 2, 0, 1).reshape(P, 8, 16))
    w = np.concatenate([x["moe_w_group"], x["moe_w_router"]], 2)
    o["wr"] = np.ascontiguousarray(w.reshape(2, KD, P, NG + NE).transpose(0, 2, 1, 3).reshape(2, P, KD * 36))
    o["gu"] = np.ascontiguousarray(x["moe_w_gate_up"].reshape(2 * NE, KD, P, 2 * FF).transpose(0, 2, 1, 3)
                                   .reshape(2 * NE, P, SLOT))
    o["dn"] = np.ascontiguousarray(x["moe_w_down"].reshape(2 * PAIRS, 2, 2, P, D).transpose(0, 3, 1, 2, 4)
                                   .reshape(2 * PAIRS, P, SLOT))
    fill = np.zeros((2 * LROW, 2), np.int32)
    fill[:, 0] = FAR
    o["lfill"] = np.ascontiguousarray(fill.reshape(P, -1))
    return o


def unpack(r):
    y = r["out_y"].transpose(2, 1, 0).reshape(T, D)
    cvp = r["out_cvp"].transpose(2, 1, 0).reshape(1, 1, 2, D)
    cvs = r["out_cvs"].reshape(P, 8, NB, 2).transpose(2, 3, 1, 0).reshape(1, NB, 2, D)
    rp = r["out_rp"].transpose(0, 2, 1, 3).reshape(1, 1, H, 256, DV)
    rs = r["out_rs"].reshape(NB, P, H, 2, DV).transpose(0, 2, 3, 1, 4).reshape(1, NB, H, 256, DV)
    mk = r["out_mk"].reshape(2, 1, NM, H, 256)
    mv = r["out_mv"].reshape(2, 1, NM, H, 256)
    return tuple(np.ascontiguousarray(v) for v in
                 (y[:TP].reshape(1, TP, D), y[TP:].reshape(NB, NS, D), cvp, cvs, rp, rs, mk, mv))


def kernel(**inputs):
    import concourse.bacc as bacc
    from concourse.bass_utils import run_bass_kernel_spmd

    x = {k: np.asarray(v) for k, v in inputs.items()}
    arrays = lay_out(x)
    nc = bacc.Bacc("TRN2", target_bir_lowering=False, num_devices=1)
    a = {n: nc.dram_tensor("in_" + n, v.shape, mybir.dt.from_np(v.dtype), kind="ExternalInput").ap()
         for n, v in arrays.items()}
    for n, shape in OUTS.items():
        a[n] = nc.dram_tensor(n, shape, F32, kind="ExternalOutput").ap()
    build(nc, a)
    r = run_bass_kernel_spmd(nc, [{"in_" + n: v for n, v in arrays.items()}], core_ids=[0])
    return unpack({n: r.results[0][n] for n in OUTS})
```
